# Optimizing a Trainium2 kernel written in Bass

```python
import jax, jax.numpy as jnp
from jax import lax
import numpy as np

D_MODEL = 1024
BATCH = 1
SEQ = 512
DEPTH = 2
DEC_BATCH = 8
DEC_SEQ = 1
PAST_LEN = 1024
PAGE_SIZE = 128

SB_HEADS = 8
SB_HEAD_DIM = 64
D_SB = SB_HEADS * SB_HEAD_DIM
Q_BLOCK = 128
SB_BIAS_INIT = -7.0
POOL_WINDOWS = (2, 4, 8, 16)
N_POOL_GROUPS = len(POOL_WINDOWS)
D_POOL = D_MODEL // 2
POOL_GD = D_POOL // N_POOL_GROUPS
POOL_HIST = max(POOL_WINDOWS) - 1
D_CONV = D_MODEL
CONV_WIDTH = 31
CONV_HIST = CONV_WIDTH - 1
N_EXPERT_GROUPS = 4
EXPERTS_PER_GROUP = 4
N_EXPERTS = N_EXPERT_GROUPS * EXPERTS_PER_GROUP
TOP_K_IN_GROUP = 2
D_EXPERT = D_MODEL // 2
D_PLE = 256
N_AB_LAYERS = (DEPTH + 1) // 2
N_C_LAYERS = DEPTH // 2
EPS = 1e-6

kernel_name = 'stickbreak_pool_conformer_hmoe_decoder_step'

def rmsnorm(x, g):
    xf = x.astype(jnp.float32)
    y = xf * lax.rsqrt(jnp.mean(xf * xf, axis=-1, keepdims=True) + EPS)
    return (y * g.astype(jnp.float32)).astype(x.dtype)

def layernorm(x, g, b):
    xf = x.astype(jnp.float32)
    mu = jnp.mean(xf, axis=-1, keepdims=True)
    xc = xf - mu
    y = xc * lax.rsqrt(jnp.mean(xc * xc, axis=-1, keepdims=True) + EPS)
    return (y * g.astype(jnp.float32) + b.astype(jnp.float32)).astype(x.dtype)

def sb_block(q, k, v, bias, q_pos, k_pos):
    z = jnp.einsum('bqhd,bkhd->bhqk', q, k, preferred_element_type=jnp.float32) * (SB_HEAD_DIM ** -0.5)
    z = z + bias.astype(jnp.float32)[None, :, None, None]
    causal = (k_pos[None, :] < q_pos[:, None])[None, None]
    log_stay = jnp.where(causal, jax.nn.log_sigmoid(-z), 0.0)
    between = lax.cumsum(log_stay, axis=3, reverse=True) - log_stay
    weight = jnp.where(causal, jnp.exp(jax.nn.log_sigmoid(z) + between), 0.0)
    return jnp.einsum('bhqk,bkhd->bqhd', weight.astype(v.dtype), v)

def sb_attention(q, k, v, bias, pos0):
    b, tq, h, dh = q.shape
    tk = k.shape[1]
    k_pos = jnp.arange(tk)
    q_pos = pos0 + jnp.arange(tq)
    if tq <= Q_BLOCK:
        return sb_block(q, k, v, bias, q_pos, k_pos)
    nb = tq // Q_BLOCK
    qb = q.reshape(b, nb, Q_BLOCK, h, dh).transpose(1, 0, 2, 3, 4)
    pb = q_pos.reshape(nb, Q_BLOCK)
    ob = lax.map(lambda a: sb_block(a[0], k, v, bias, a[1], k_pos), (qb, pb))
    return ob.transpose(1, 0, 2, 3, 4).reshape(b, tq, h, dh)

def multiscale_pool(u, hist, pos0):
    t = u.shape[1]
    xp = jnp.concatenate([hist.astype(u.dtype), u], axis=1)
    xf = xp.astype(jnp.float32)
    cs = jnp.concatenate([jnp.zeros_like(xf[:, :1]), jnp.cumsum(xf, axis=1)], axis=1)
    pos = pos0 + jnp.arange(t)
    outs = []
    for g, w in enumerate(POOL_WINDOWS):
        c = slice(g * POOL_GD, (g + 1) * POOL_GD)
        s = cs[:, POOL_HIST + 1:POOL_HIST + 1 + t, c] - cs[:, POOL_HIST + 1 - w:POOL_HIST + 1 - w + t, c]
        cnt = jnp.minimum(pos + 1, w).astype(jnp.float32)
        outs.append(s / cnt[None, :, None])
    pooled = jnp.concatenate(outs, axis=-1) - u.astype(jnp.float32)
    return pooled.astype(u.dtype), xp[:, -POOL_HIST:]

def conformer_conv(h, hist, w_in, w_dw, b_dw, ln_g, ln_b, w_out):
    a, g = jnp.split(h @ w_in, 2, axis=-1)
    u = a * jax.nn.sigmoid(g)
    up = jnp.concatenate([hist.astype(u.dtype), u], axis=1)
    y = lax.conv_general_dilated(up, w_dw[:, None, :].astype(up.dtype), window_strides=(1,), padding='VALID',
                                 dimension_numbers=('NWC', 'WIO', 'NWC'), feature_group_count=D_CONV) + b_dw
    y = jax.nn.silu(layernorm(y, ln_g, ln_b))
    return y @ w_out, up[:, -CONV_HIST:]

def hier_moe(x, w_rg, b_rg, w_re, b_re, w_gate, w_up, w_down):
    shp = x.shape
    xf = x.reshape(-1, D_MODEL)
    n = xf.shape[0]
    g_logits = (xf @ w_rg + b_rg).astype(jnp.float32)
    g_prob = jax.nn.softmax(g_logits, axis=-1)
    _, g_idx = lax.top_k(g_logits, 1)
    p_group = jnp.take_along_axis(g_prob, g_idx, axis=-1)
    e_logits = (xf @ w_re + b_re).astype(jnp.float32).reshape(n, N_EXPERT_GROUPS, EXPERTS_PER_GROUP)
    e_in = jnp.take_along_axis(e_logits, g_idx[:, :, None], axis=1)[:, 0]
    e_val, e_idx = lax.top_k(e_in, TOP_K_IN_GROUP)
    w_sel = jax.nn.softmax(e_val, axis=-1) * p_group
    expert_id = g_idx * EXPERTS_PER_GROUP + e_idx
    combine = jnp.sum(jax.nn.one_hot(expert_id, N_EXPERTS, dtype=jnp.float32) * w_sel[..., None], axis=1).astype(x.dtype)
    y = jnp.zeros_like(xf)
    for e in range(N_EXPERTS):
        hid = jax.nn.silu(xf @ w_gate[e]) * (xf @ w_up[e])
        y = y + combine[:, e:e + 1] * (hid @ w_down[e])
    return y.reshape(shp)

def per_layer_embedding(h, p, w_ple, w_pg, b_pg, g_pg):
    gate = jax.nn.sigmoid((rmsnorm(h, g_pg) @ w_pg + b_pg).astype(jnp.float32))
    return h + (gate * (p @ w_ple).astype(jnp.float32)).astype(h.dtype)

def trunk(x, p, pos0, past_k, past_v, pool_hist, conv_hist, prm):
    b, t, _ = x.shape
    h = x
    new_k, new_v, new_pool, new_conv = [], [], [], []
    for i in range(DEPTH):
        hn = rmsnorm(h, prm['norm_mix'][i])
        li = i // 2
        if i % 2 == 0:
            proj = hn @ prm['w_in_ab'][li]
            q = proj[..., :D_SB].reshape(b, t, SB_HEADS, SB_HEAD_DIM)
            k = proj[..., D_SB:2 * D_SB].reshape(b, t, SB_HEADS, SB_HEAD_DIM)
            v = proj[..., 2 * D_SB:3 * D_SB].reshape(b, t, SB_HEADS, SB_HEAD_DIM)
            u = proj[..., 3 * D_SB:]
            k_all = jnp.concatenate([past_k[li].astype(k.dtype), k], axis=1)
            v_all = jnp.concatenate([past_v[li].astype(v.dtype), v], axis=1)
            o_sb = sb_attention(q, k_all, v_all, prm['sb_bias'][li], pos0).reshape(b, t, D_SB)
            pooled, pool_state = multiscale_pool(u, pool_hist[li], pos0)
            o_pool = jnp.einsum('btgc,gcd->btgd', pooled.reshape(b, t, N_POOL_GROUPS, POOL_GD),
                                prm['w_pool'][li]).reshape(b, t, D_POOL) * prm['pool_scale'][li]
            mix = jnp.concatenate([o_sb, o_pool], axis=-1) @ prm['w_out_ab'][li]
            new_k.append(k)
            new_v.append(v)
            new_pool.append(pool_state)
        else:
            mix, conv_state = conformer_conv(hn, conv_hist[li], prm['w_in_c'][li], prm['w_dw'][li], prm['b_dw'][li],
                                             prm['ln_g_c'][li], prm['ln_b_c'][li], prm['w_out_c'][li])
            new_conv.append(conv_state)
        h = h + mix
        h = h + hier_moe(rmsnorm(h, prm['norm_ffn'][i]), prm['w_rg'][i], prm['b_rg'][i], prm['w_re'][i], prm['b_re'][i],
                         prm['w_gate_e'][i], prm['w_up_e'][i], prm['w_down_e'][i])
        h = per_layer_embedding(h, p[i], prm['w_ple'][i], prm['w_ple_gate'][i], prm['b_ple_gate'][i], prm['g_ple_gate'][i])
    y = rmsnorm(h, prm['norm_final'])
    return y, jnp.stack(new_k), jnp.stack(new_v), jnp.stack(new_pool), jnp.stack(new_conv)

def setup_inputs(seed: int = 0) -> dict:
    key = jax.random.key(seed)
    ks = iter(jax.random.split(key, 48))

    def nrm(shape, scale=1.0):
        return jax.random.normal(next(ks), shape, jnp.float32) * scale

    n_pages = PAST_LEN // PAGE_SIZE
    n_used = DEC_BATCH * n_pages
    n_phys = n_used + n_used // 4
    page_table = jax.random.permutation(next(ks), n_phys)[:n_used].reshape(DEC_BATCH, n_pages).astype(jnp.int32)
    return {
        'x_prompt': nrm((BATCH, SEQ, D_MODEL)),
        'x_sample': nrm((DEC_BATCH, DEC_SEQ, D_MODEL)),
        'p_prompt': nrm((DEPTH, BATCH, SEQ, D_PLE)),
        'p_sample': nrm((DEPTH, DEC_BATCH, DEC_SEQ, D_PLE)),
        'cache_k': nrm((N_AB_LAYERS, n_phys, PAGE_SIZE, SB_HEADS, SB_HEAD_DIM)),
        'cache_v': nrm((N_AB_LAYERS, n_phys, PAGE_SIZE, SB_HEADS, SB_HEAD_DIM)),
        'state_pool': nrm((N_AB_LAYERS, DEC_BATCH, POOL_HIST, D_POOL)),
        'state_conv': nrm((N_C_LAYERS, DEC_BATCH, CONV_HIST, D_CONV), 0.5),
        'page_table': page_table,
        'norm_mix': 1.0 + nrm((DEPTH, D_MODEL), 0.02),
        'norm_ffn': 1.0 + nrm((DEPTH, D_MODEL), 0.02),
        'norm_final': 1.0 + nrm((D_MODEL,), 0.02),
        'w_in_ab': nrm((N_AB_LAYERS, D_MODEL, 3 * D_SB + D_POOL), D_MODEL ** -0.5),
        'sb_bias': SB_BIAS_INIT + nrm((N_AB_LAYERS, SB_HEADS), 0.5),
        'w_pool': nrm((N_AB_LAYERS, N_POOL_GROUPS, POOL_GD, POOL_GD), POOL_GD ** -0.5),
        'pool_scale': 1.0 + nrm((N_AB_LAYERS, D_POOL), 0.02),
        'w_out_ab': nrm((N_AB_LAYERS, D_SB + D_POOL, D_MODEL), (D_SB + D_POOL) ** -0.5),
        'w_in_c': nrm((N_C_LAYERS, D_MODEL, 2 * D_CONV), D_MODEL ** -0.5),
        'w_dw': nrm((N_C_LAYERS, CONV_WIDTH, D_CONV), CONV_WIDTH ** -0.5),
        'b_dw': nrm((N_C_LAYERS, D_CONV), 0.02),
        'ln_g_c': 1.0 + nrm((N_C_LAYERS, D_CONV), 0.02),
        'ln_b_c': nrm((N_C_LAYERS, D_CONV), 0.02),
        'w_out_c': nrm((N_C_LAYERS, D_CONV, D_MODEL), D_CONV ** -0.5),
        'w_rg': nrm((DEPTH, D_MODEL, N_EXPERT_GROUPS), D_MODEL ** -0.5),
        'b_rg': nrm((DEPTH, N_EXPERT_GROUPS), 0.01),
        'w_re': nrm((DEPTH, D_MODEL, N_EXPERTS), D_MODEL ** -0.5),
        'b_re': nrm((DEPTH, N_EXPERTS), 0.01),
        'w_gate_e': nrm((DEPTH, N_EXPERTS, D_MODEL, D_EXPERT), D_MODEL ** -0.5),
        'w_up_e': nrm((DEPTH, N_EXPERTS, D_MODEL, D_EXPERT), D_MODEL ** -0.5),
        'w_down_e': nrm((DEPTH, N_EXPERTS, D_EXPERT, D_MODEL), D_EXPERT ** -0.5),
        'w_ple': nrm((DEPTH, D_PLE, D_MODEL), D_PLE ** -0.5),
        'w_ple_gate': nrm((DEPTH, D_MODEL, D_MODEL), D_MODEL ** -0.5),
        'b_ple_gate': nrm((DEPTH, D_MODEL), 0.02),
        'g_ple_gate': 1.0 + nrm((DEPTH, D_MODEL), 0.02),
    }

def reference(x_prompt, x_sample, p_prompt, p_sample, cache_k, cache_v, state_pool, state_conv, page_table,
              norm_mix, norm_ffn, norm_final, w_in_ab, sb_bias, w_pool, pool_scale, w_out_ab,
              w_in_c, w_dw, b_dw, ln_g_c, ln_b_c, w_out_c,
              w_rg, b_rg, w_re, b_re, w_gate_e, w_up_e, w_down_e,
              w_ple, w_ple_gate, b_ple_gate, g_ple_gate):
    prm = dict(norm_mix=norm_mix, norm_ffn=norm_ffn, norm_final=norm_final, w_in_ab=w_in_ab, sb_bias=sb_bias,
               w_pool=w_pool, pool_scale=pool_scale, w_out_ab=w_out_ab, w_in_c=w_in_c, w_dw=w_dw, b_dw=b_dw,
               ln_g_c=ln_g_c, ln_b_c=ln_b_c, w_out_c=w_out_c, w_rg=w_rg, b_rg=b_rg, w_re=w_re, b_re=b_re,
               w_gate_e=w_gate_e, w_up_e=w_up_e, w_down_e=w_down_e, w_ple=w_ple, w_ple_gate=w_ple_gate,
               b_ple_gate=b_ple_gate, g_ple_gate=g_ple_gate)
    bp = x_prompt.shape[0]
    n_ab = w_in_ab.shape[0]
    n_c = w_in_c.shape[0]
    empty_kv = jnp.zeros((n_ab, bp, 0, SB_HEADS, SB_HEAD_DIM), x_prompt.dtype)
    zero_pool = jnp.zeros((n_ab, bp, POOL_HIST, D_POOL), x_prompt.dtype)
    zero_conv = jnp.zeros((n_c, bp, CONV_HIST, D_CONV), x_prompt.dtype)
    y_prompt, k_prompt, v_prompt, pool_prompt, conv_prompt = trunk(
        x_prompt, p_prompt, 0, empty_kv, empty_kv, zero_pool, zero_conv, prm)
    db, n_pages = page_table.shape
    past_len = n_pages * PAGE_SIZE
    past_k = cache_k[:, page_table].reshape(n_ab, db, past_len, SB_HEADS, SB_HEAD_DIM)
    past_v = cache_v[:, page_table].reshape(n_ab, db, past_len, SB_HEADS, SB_HEAD_DIM)
    y_sample, k_sample, v_sample, pool_sample, conv_sample = trunk(
        x_sample, p_sample, past_len, past_k, past_v, state_pool, state_conv, prm)
    return (y_prompt, y_sample, k_prompt, v_prompt, pool_prompt, conv_prompt, k_sample, v_sample, pool_sample, conv_sample)


_drawn_inputs = setup_inputs


def setup_inputs(seed=0):
    import zlib

    import numpy as np

    out = dict(_drawn_inputs(seed))
    spreads = {}
    factors = {'norm_final': 8.038,
     'sb_bias': 27.992,
     'ln_g_c': 3.764,
     'ln_b_c': 3.519,
     'b_rg': 4.049,
     'b_re': 5.4,
     'b_ple_gate': 23.265,
     'g_ple_gate': 22.88,
     'cache_k': 8.0,
     'cache_v': 8.0}
    for name, (base, spread) in spreads.items():
        noise = np.random.default_rng([zlib.crc32(name.encode()), seed]).standard_normal(out[name].shape)
        drawn = base * np.exp(spread * noise) if base else spread * noise
        out[name] = __import__('jax').numpy.asarray(drawn.astype(out[name].dtype))
    for name, factor in factors.items():
        out[name] = (out[name] * factor).astype(out[name].dtype)
    return out
```

```python
from contextlib import ExitStack

import concourse.bass as bass
from concourse import mybir

ALU = mybir.AluOpType
ACT = mybir.ActivationFunctionType
F32 = mybir.dt.float32
I32 = mybir.dt.int32
AX = mybir.AxisListType.X

P = 128
D = 1024
KT = D // P
TP, TS = 512, 8
T = TP + TS
HALF = T // 2
RT, NRT = 104, 5
SBH, DH = 8, 64
PAGES, PAGE = 8, 128
N_PHYS = 80
DPOOL, PW = 512, (2, 4, 8, 16)
HIST = 15
CW, CHIST = 31, 30
NG, NPG = 4, 4
NE = NG * NPG
F = 512
FT = F // P
DPLE = 256
EPS = 1e-6
CAP = 128
BLK = 5
UNUSED = float(1 << 20)
RING = 6
PAD = 16
CPAD = 30
CONV_DVE = 5
MULT = 1.0 / D

G_MIX, G_FFN, G_FIN, B_DW, LN_G, LN_B, B_PG, G_PG, P_SC = 0, 16, 32, 40, 48, 56, 64, 80, 96
N_PRM = 100


def unit_plan():
    units = [("w_in_ab", c) for c in range(4)]
    units += [("k", b) for b in range(TS)] + [("v", b) for b in range(TS)]
    units += [("w_out_ab", c) for c in range(2)]
    first_expert = []
    for layer in range(2):
        if layer:
            units += [("w_in_c", c) for c in (0, 2, 1, 3)] + [("w_out_c", c) for c in range(2)]
        first_expert.append(len(units))
        units += [("gate", layer, 0), ("up", layer, 0)]
        for e in range(1, NE):
            units += [("gate", layer, e), ("up", layer, e), ("down", layer, e - 1)]
        units += [("down", layer, NE - 1)]
        units += [("w_ple", layer), ("w_pg", layer, 0), ("w_pg", layer, 1)]
    return units, first_expert


UNITS, FIRST_EXPERT = unit_plan()
UNIT = {u: n for n, u in enumerate(UNITS)}


def is_cache(u):
    return u[0] in "kv"


def landed_count(n):
    kind = is_cache(UNITS[n])
    return sum(is_cache(UNITS[m]) == kind for m in range(n % RING, n + 1, RING))


def dense_plan():
    order = [("x", i, "dve") for i in range(5)]

    def norm(i):
        order.append(("norm", i, "act"))

    def moe(layer):
        order.append(("logits", layer, "dve"))
        order.extend(("rows", (layer, i), "act") for i in range(NRT))
        order.append(("rank", layer, "dve"))
        order.append(("table", layer, "dve"))
        order.extend(("combine", (layer, d), "dve") for d in range(KT))

    def ple(layer):
        order.extend(("pT", (layer, i), "act") for i in range(2))
        for m in range(KT):
            order.append(("pgate", (layer, m), "act"))
            order.append(("pvalue", (layer, m), "dve"))

    norm(0)
    order += [("q", m, "act") for m in range(4)] + [("k", m, "dve") for m in range(4)]
    order += [("v", i, "act") for i in range(3)] + [("u", m, "dve") for m in range(4)]
    order += [("qrow", 0, "act")] + [("krow", i, "dve") for i in range(3)] + [("urow", 0, "dve")]
    order += [("cs", 0, "dve"), ("vs", 0, "dve")]
    order += [("poolproj", m, "dve") for m in range(4)] + [("wout", m, "dve") for m in range(KT)]
    norm(1)
    moe(0)
    norm(2)
    ple(0)
    norm(3)
    order += [("chist", i, "dve") for i in range(2)]
    for m in range(KT):
        order += [("cg", m, "act"), ("ca", m, "dve")]
    order += [("crow", 0, "act"), ("csrow", 0, "act")]
    order += [("conv", m, "act") for m in range(CONV_DVE, KT)]
    order += [("mean", 0, "act"), ("var", 0, "act")]
    order += [("woutc", m, "dve") for m in range(KT)]
    norm(4)
    moe(1)
    norm(5)
    ple(1)
    norm(6)
    order += [("y", i, "act") for i in range(5)]
    jobs, drains = {}, {"act": 0, "dve": 0}
    for n, (name, i, engine) in enumerate(order):
        drains[engine] += 1
        jobs[(name, i)] = (n, engine, drains[engine])
    return jobs


JOBS = dense_plan()
BY_NUMBER = sorted(JOBS.values())


def decoder_step(nc, a, out):
    with ExitStack() as ctx:
        def sb(name, shape, dt=F32):
            return ctx.enter_context(nc.sbuf_tensor(name, shape, dt))

        def sem(name):
            return ctx.enter_context(nc.semaphore(name))

        x_rows = [nc.dram_tensor(f"x_rows{i}", (T, D), F32, kind="Internal").ap() for i in range(2)]
        y_rows = [nc.dram_tensor(f"y_rows{i}", (2 * T, D), F32, kind="Internal").ap() for i in range(2)]
        q_rows = nc.dram_tensor("q_rows", (TS, 512), F32, kind="Internal").ap()

        ps = ctx.enter_context(nc.psum_tensor("ps", [P, 8, 512], F32))
        ps_flat = ps[:].rearrange("p a b -> p (a b)")

        def slot(n):
            return ps[:, 2 * (n % 4):2 * (n % 4) + 2, :]

        hT = sb("hT", [P, KT, T])
        xnT = sb("xnT", [P, KT, T])
        ring = sb("ring", [P, RING, 4096])
        sq = sb("sq", [P, 2, 528])
        rms = sb("rms", [P, T])
        rstd = sb("rstd", [P, T])
        ident = sb("ident", [P, P])
        tri = sb("tri", [P, P])
        before = sb("before", [P, P])
        ones = sb("ones", [P, P])
        prm = sb("prm", [P, N_PRM])
        wdw = sb("wdw", [P, KT, CW])
        wpool = sb("wpool", [P, 4, P])
        eps = sb("eps", [P, 1])
        one = sb("one", [P, 1])
        sbb = sb("sbb", [P, SBH])
        cfix = sb("cfix", [P, 4, 16])
        tab_i = sb("tab_i", [P, 2, NE * BLK], I32)
        idx = sb("idx", [P, 2, 2], I32)
        flag = sb("flag", [1, 1], I32)
        wts = sb("wts", [RT, 2, NRT])
        pt = sb("pt", [1, TS * PAGES], I32)
        arena = sb("arena", [P, 16100])

        class Arena:
            def __init__(self, at=0):
                self.at = at

            def __call__(self, *shape, rows=P):
                size = 1
                for s in shape:
                    size *= s
                v = arena[0:rows, self.at:self.at + size]
                self.at += size
                assert self.at <= 16100, self.at
                if len(shape) == 2:
                    v = v.rearrange("p (a b) -> p a b", a=shape[0])
                if len(shape) == 3:
                    v = v.rearrange("p (a b c) -> p a b c", a=shape[0], b=shape[1])
                return v

        ar = Arena()
        x_tok = ar(4, D)
        x_smp = ar(D, rows=TS)
        prm_rows = ar(P, rows=N_PRM)
        dw_rows = ar(D, rows=CW)
        ar = Arena()
        qT = ar(4, T)
        kT = ar(4, T)
        v_tok = ar(NRT, 512)
        up = ar(4, PAD + T)
        spans = ar.at
        zs = ar(2, 1280)
        ex = ar(2, 1280)
        qbc = ar(2, 512)
        zz = ar(TS, PAGES, SBH)
        zl = ar(TS, PAGES, SBH)
        zr = qbc.rearrange("p a (b g h) -> p (a b) g h", b=TS, g=PAGES)[:, 0:TS]
        ar = Arena(spans)
        k_tok = ar(NRT, 512)
        q_row = ar(2, 512, rows=TS)
        u_row = ar(512, rows=HIST)
        hist_rows = ar(512, rows=TS * HIST)
        hist = ar(4, TS, HIST + 1)
        ar = Arena()
        xg = ar(2, D)
        xgT = ar(KT, CAP)
        sil = ar(F)
        hid = ar(F)
        hidT = ar(FT, CAP)
        yo = ar(2, D)
        xr = ar(2, D, rows=RT)
        wr = ar(KT, 20)
        br = ar(20, rows=RT)
        lg = ar(NRT, 20, rows=RT)
        rs = ar(40, NRT * 4, rows=RT)
        m1 = ar(NRT, NG, NPG, rows=RT)
        m2 = ar(NRT, NG, NPG, rows=RT)
        mt = ar(NRT, NG, NPG, rows=RT)
        cnt = ar(NRT, NE, rows=RT)
        sel_c = ar(10, CAP, rows=RT)
        sel_b = ar(10, NE * BLK, rows=RT)
        iot = ar(CAP, rows=RT)
        io16 = ar(NE, rows=RT)
        prio = ar(NPG, rows=RT)
        vals = ar(2, NRT, rows=RT)
        tabf = ar(3, NE * BLK)
        ar = Arena()
        yg = ar(NRT, 2 * D, rows=RT)
        ar = Arena()
        p_tok = ar(4, DPLE)
        p_smp = ar(DPLE, rows=TS)
        pT = ar(2, T)
        sig = ar(2, T)
        gv = ar(2, T)
        ar = Arena()
        cu = ar(KT, CPAD + TP)
        chs = ar(KT, TS * CW)
        acc = ar(KT, T)
        ch_rows = ar(2, D, rows=120)
        diag = ar(4, P)
        csig = ar(2, T)
        c_row, cs_row = ch_rows[0:CHIST, 0, :], ch_rows[0:TS, 1, :]
        cprod = ar(TS * CW)
        ar = Arena()
        y_tok = ar(2, D)

        s_const = sem("s_const")
        s_in = sem("s_in")
        s_in2 = sem("s_in2")
        s_wland = [sem(f"s_wland{i}") for i in range(RING)]
        s_cland = [sem(f"s_cland{i}") for i in range(RING)]
        s_vused = sem("s_vused")
        s_kused = sem("s_kused")
        s_filled = sem("s_filled")
        s_drained = {"act": sem("s_drained_act"), "dve": sem("s_drained_dve")}
        s_dve = sem("s_dve")
        s_act = sem("s_act")
        s_pool = sem("s_pool")
        s_sq = sem("s_sq")
        s_squsd = sem("s_squsd")
        s_xn = sem("s_xn")
        s_h = sem("s_h")
        s_out = sem("s_out")
        n_out = [0]

        s_pt = sem("s_pt")
        s_qrow = sem("s_qrow")
        s_qbc = [sem(f"s_qbc{i}") for i in range(2)]
        s_kq = sem("s_kq")
        s_hist, s_upz, s_cuz = sem("s_hist"), sem("s_upz"), sem("s_cuz")
        s_stored = sem("s_stored")
        s_zf, s_zs, s_ab, s_ln = sem("s_zf"), sem("s_zs"), sem("s_ab"), sem("s_ln")
        s_sp, s_spm, s_cf, s_dd = sem("s_sp"), sem("s_spm"), sem("s_cf"), sem("s_dd")
        s_we, s_wm, s_pv, s_ot = sem("s_we"), sem("s_wm"), sem("s_pv"), sem("s_ot")
        s_zv, s_za, s_zw = sem("s_zv"), sem("s_za"), sem("s_zw")
        s_pooled, s_opool = sem("s_pooled"), sem("s_opool")
        s_rin = sem("s_rin")
        s_rc = sem("s_rc")
        s_cnt, s_sel, s_tab = sem("s_cnt"), sem("s_sel"), sem("s_tab")
        s_ri, s_ro = sem("s_ri"), sem("s_ro")
        s_xr = [sem(f"s_xr{i}") for i in range(2)]
        s_xg = [sem(f"s_xg{i}") for i in range(2)]
        s_idx, s_idy = sem("s_idx"), sem("s_idy")
        s_xtf, s_xt = sem("s_xtf"), sem("s_xt")
        s_gf, s_uf, s_sil, s_hid = sem("s_gf"), sem("s_uf"), sem("s_sil"), sem("s_hid")
        s_htf, s_ht, s_df, s_y = sem("s_htf"), sem("s_ht"), sem("s_df"), sem("s_y")
        s_ys = [sem(f"s_ys{i}") for i in range(2)]
        s_yg = [sem(f"s_yg{i}") for i in range(NRT)]
        s_yc = sem("s_yc")
        ov = [{k: sem(f"s_ov{layer}_{k}") for k in
               ("land", "eused", "idx", "xg", "xtf", "xt", "guf", "sil", "hid", "htf", "ht", "df", "y", "ys")}
              for layer in range(2)]
        s_pin = [sem(f"s_pin{i}") for i in range(2)]
        s_pT, s_sig = sem("s_pT"), sem("s_sig")
        s_cin, s_chs = sem("s_cin"), sem("s_chs")
        s_csig, s_cu = sem("s_csig"), sem("s_cu")
        s_crow = sem("s_crow")
        s_diag, s_dused = sem("s_diag"), sem("s_dused")
        s_acc, s_xc, s_lnx, s_silu = sem("s_acc"), sem("s_xc"), sem("s_lnx"), sem("s_silu")
        s_yt = [sem(f"s_yt{i}") for i in range(2)]
        s_cvf = sem("s_cvf")

        def unit(n):
            return ring[:, n % RING, :]

        def w_view(n):
            return unit(n).rearrange("p (k c) -> p k c", k=KT)

        def fill_wait(pe, name, i):
            n = JOBS[(name, i)][0]
            if n >= 4:
                _, engine, count = BY_NUMBER[n - 4]
                pe.wait_ge(s_drained[engine], count)
            return slot(n)

        def drain_wait(eng, name, i):
            n = JOBS[(name, i)][0]
            eng.wait_ge(s_filled, n + 1)
            return slot(n)

        def all_drained(pe, name, i):
            upto = JOBS[(name, i)][0]
            for engine in ("act", "dve"):
                counts = [c for n, e, c in BY_NUMBER[: upto + 1] if e == engine]
                pe.wait_ge(s_drained[engine], counts[-1])

        def unit_wait(eng, n):
            if is_cache(UNITS[n]):
                eng.wait_ge(s_cland[n % RING], 16 * PAGES * landed_count(n))
            else:
                eng.wait_ge(s_wland[n % RING], 16 * landed_count(n))

        def h_wait(eng, upd, k):
            if upd == "x":
                eng.wait_ge(s_drained["dve"], JOBS[("x", 4)][2])
            elif upd[:3] == "ple":
                eng.wait_ge(s_h, 8 * int(upd[3]) + k + 1)
            else:
                job = ("combine", (int(upd[3]), k)) if upd[:3] == "moe" else (upd, k)
                eng.wait_ge(s_drained["dve"], JOBS[job][2])

        def used_wait(eng, n):
            u = UNITS[n]
            if u[0] == "k":
                eng.wait_ge(s_kused, u[1] + 1)
            elif u[0] == "v":
                eng.wait_ge(s_vused, u[1] + 1)
            elif u[0] in ("gate", "up", "down"):
                eng.wait_ge({"gate": s_gf, "up": s_uf, "down": s_df}[u[0]], NE * u[1] + u[2] + 1)
            else:
                last = {"w_in_ab": lambda c: ("qkvu"[c], 2 if c == 2 else 3), "w_out_ab": lambda c: ("wout", 4 * c + 3),
                        "w_in_c": lambda c: ("ca", 4 * (c % 2) + 3), "w_out_c": lambda c: ("woutc", 4 * c + 3),
                        "w_ple": lambda layer: ("pvalue", (layer, KT - 1)),
                        "w_pg": lambda layer, c: ("pgate", (layer, 4 * c + 3))}[u[0]](*u[1:])
                eng.wait_ge(s_filled, JOBS[last][0] + 1)

        def stored(ins):
            n_out[0] += 1
            ins.then_inc(s_out, 16)

        def unit_source(u):
            if u[0] in ("w_in_ab", "w_out_ab", "w_in_c", "w_out_c"):
                return a[u[0]][0].rearrange("(k p) c -> p k c", p=P)[:, :, u[1] * 512:(u[1] + 1) * 512]
            if u[0] == "w_ple":
                return a["w_ple"][u[1]].rearrange("(k p) c -> p k c", p=P)
            return a["w_ple_gate"][u[1]].rearrange("(k p) c -> p k c", p=P)[:, :, u[2] * 512:(u[2] + 1) * 512]

        def ple_view(n):
            return unit(n)[:, 0:2048].rearrange("p (k c) -> p k c", k=2)

        block = ctx.enter_context(nc.Block())

        @block.sync
        def _(sp):
            def free_wait(n):
                if n >= RING:
                    used_wait(sp, n - RING)

            def load(n):
                free_wait(n)
                src = unit_source(UNITS[n])
                dst = ple_view(n) if UNITS[n][0] == "w_ple" else w_view(n)
                sp.dma_start(dst, src).then_inc(s_wland[n % RING], 16)

            sp.dma_start(x_tok, a["x_prompt"][0].rearrange("(i p) d -> p i d", p=P)).then_inc(s_in, 16)
            sp.dma_start(x_smp, a["x_sample"][:, 0, :]).then_inc(s_in, 16)
            load(0)
            sp.dma_start(pt[:], a["page_table"].rearrange("b n -> (b n)").unsqueeze(0)).then_inc(s_pt, 16)
            for n in range(1, 4):
                load(n)

            sp.wait_ge(s_pt, 16)
            for kind in "kv":
                pages = a[f"cache_{kind}"][0].rearrange("n s h d -> n s (h d)")
                for b in range(TS):
                    n = UNIT[(kind, b)]
                    free_wait(n)
                    dst = unit(n).rearrange("p (g c) -> p g c", g=PAGES)
                    for g in range(PAGES):
                        page = sp.value_load(pt[0:1, b * PAGES + g:b * PAGES + g + 1], min_val=0, max_val=N_PHYS - 1)
                        sp.dma_start(dst[:, g:g + 1, :],
                                     pages[bass.ds(page, 1)].rearrange("a s c -> s a c")
                                     ).then_inc(s_cland[n % RING], 16)
            load(UNIT[("w_out_ab", 0)])
            load(UNIT[("w_out_ab", 1)])

            for layer in range(2):
                if layer:
                    for u in (("w_in_c", 0), ("w_in_c", 2), ("w_in_c", 1), ("w_in_c", 3),
                              ("w_out_c", 0), ("w_out_c", 1)):
                        load(UNIT[u])
                u0 = FIRST_EXPERT[layer]
                gate, upw, down = (a[w][layer].rearrange("e (k p) c -> p (e k) c", p=P)
                                   for w in ("w_gate_e", "w_up_e", "w_down_e"))

                def expert_part(w, e, s):
                    k = w.shape[1] // NE
                    return ring[:, s, :].rearrange("p (k c) -> p k c", k=k), w[:, bass.ds(e * k, k), :]

                def expert_load(n, w, e):
                    sp.dma_start(*expert_part(w, e, n % RING)).then_inc(s_wland[n % RING], 16)

                def load_step(e):
                    n = u0 + 3 * e - 1
                    for i, (w, x) in enumerate(((gate, e), (upw, e), (down, e - 1))):
                        free_wait(n + i)
                        expert_load(n + i, w, x)

                def load_step_in_loop(e0, e):
                    n = u0 + 3 * e0 - 1
                    for i, (w, x, done) in enumerate(((gate, e, s_gf), (upw, e, s_uf), (down, e - 1, s_df))):
                        sp.wait_ge(done, NE * layer + x - 1)
                        expert_load(n + i, w, x)

                for n, w in ((u0, gate), (u0 + 1, upw)):
                    free_wait(n)
                    expert_load(n, w, 0)
                load_step(1)
                load_step(2)
                with sp.Fori(0, 6) as j:
                    load_step_in_loop(3, 2 * j + 3)
                    load_step_in_loop(4, 2 * j + 4)
                load_step(15)
                free_wait(u0 + 47)
                expert_load(u0 + 47, down, 15)

                sp.wait_ge(s_tab, 2 * layer + 2)
                more = sp.value_load(flag[0:1, 0:1], min_val=0, max_val=1)
                with sp.If(more > 0):
                    used_wait(sp, u0 + 47)
                    with sp.Fori(0, NE) as e:
                        sp.wait_ge(ov[layer]["eused"], e)
                        for s, w in enumerate((gate, upw, down)):
                            sp.dma_start(*expert_part(w, e, s)).then_inc(ov[layer]["land"], 16)
                    sp.wait_ge(ov[layer]["eused"], NE)
                for u in (("w_ple", layer), ("w_pg", layer, 0), ("w_pg", layer, 1)):
                    load(UNIT[u])

        @block.gpsimd
        def _(pool):
            steps = [0]
            last_token, last_result = pool.to_reg(T - 1), pool.to_reg(2 * T - 1)

            def wait_alone(semaphore, count):
                if not isinstance(count, int):
                    count = pool.to_reg(count)
                pool.wait_ge(s_const, 1)
                pool.wait_ge(semaphore, count)

            def link(ins):
                steps[0] += 1
                ins.then_inc(s_pool, 1)
                pool.wait_ge(s_pool, steps[0])

            for name, row in (("norm_mix", G_MIX), ("norm_ffn", G_FFN), ("b_ple_gate", B_PG), ("g_ple_gate", G_PG)):
                pool.dma_start(prm_rows[row:row + 16, :], a[name].rearrange("l (k p) -> (l k) p", p=P)).then_inc(s_in2, 16)
            pool.dma_start(prm_rows[G_FIN:G_FIN + 8, :], a["norm_final"].rearrange("(k p) -> k p", p=P)).then_inc(s_in2, 16)
            for name, row, n in (("b_dw", B_DW, 8), ("ln_g_c", LN_G, 8), ("ln_b_c", LN_B, 8), ("pool_scale", P_SC, 4)):
                pool.dma_start(prm_rows[row:row + n, :], a[name][0].rearrange("(k p) -> k p", p=P)).then_inc(s_in2, 16)
            pool.dma_start(dw_rows, a["w_dw"][0]).then_inc(s_in2, 16)
            pool.dma_start(sbb[:], a["sb_bias"][0].partition_broadcast(P)).then_inc(s_in2, 16)
            pool.dma_start(wpool[:], a["w_pool"][0].rearrange("g c d -> c g d")).then_inc(s_in2, 16)

            link(pool.memset(ones[:], 1.0))
            link(pool.memset(ident[:], 0.0))
            link(pool.affine_select(out=ident[:], in_=ident[:], compare_op=ALU.not_equal, fill=1.0, base=0,
                                    pattern=[[-1, P]], channel_multiplier=1))
            link(pool.affine_select(out=tri[:], in_=ones[:], compare_op=ALU.is_ge, fill=0.0, base=0,
                                    pattern=[[-1, P]], channel_multiplier=1))
            link(pool.affine_select(out=before[:], in_=ones[:], compare_op=ALU.is_gt, fill=0.0, base=0,
                                    pattern=[[1, P]], channel_multiplier=-1))
            link(pool.memset(eps[:], EPS))
            link(pool.memset(one[:], 1.0))
            link(pool.iota(cfix[:], [[0, 4], [1, 16]], base=1, channel_multiplier=0,
                           allow_small_or_imprecise_dtypes=True))
            pool.memset(idx[:], 0).then_inc(s_const, 1)

            stored(pool.dma_start(out["pool_sample"][0, :, 0:HIST - 1, :], a["state_pool"][0, :, 1:HIST, :]))
            stored(pool.dma_start(out["conv_sample"][0, :, 0:CHIST - 1, :], a["state_conv"][0, :, 1:CHIST, :]))

            pool.wait_ge(s_filled, JOBS[("x", 4)][0] + 1)
            pool.memset(up[:, :, 0:PAD], 0.0).then_inc(s_upz, 1)
            pool.dma_start(hist_rows, a["state_pool"][0].rearrange("b r c -> (b r) c")).then_inc(s_hist, 16)

            pool.wait_ge(s_drained["act"], JOBS[("qrow", 0)][2])
            pool.dma_start(q_rows, q_row[:, 0, :]).then_inc(s_qrow, 16)
            stored(pool.dma_start(out["pool_sample"][0, :, HIST - 1, :], q_row[:, 1, :]))
            stored(pool.dma_start(out["v_prompt"][0, 0].rearrange("(i p) h d -> p i (h d)", p=P), v_tok[:, 0:4, :]))
            stored(pool.dma_start(out["v_sample"][0, :, 0].rearrange("b h d -> b (h d)"), v_tok[0:TS, 4, :]))
            pool.wait_ge(s_drained["dve"], JOBS[("krow", 2)][2])
            stored(pool.dma_start(out["k_prompt"][0, 0].rearrange("(i p) h d -> p i (h d)", p=P), k_tok[:, 0:4, :]))
            stored(pool.dma_start(out["k_sample"][0, :, 0].rearrange("b h d -> b (h d)"), k_tok[0:TS, 4, :]))
            pool.wait_ge(s_drained["dve"], JOBS[("urow", 0)][2])
            stored(pool.dma_start(out["pool_prompt"][0, 0], u_row))
            pool.wait_ge(s_out, 16 * n_out[0])
            pool.wait_ge(s_qrow, 16)
            pool.sem_inc(s_stored, 1)

            def load_query(b):
                if b >= 2:
                    pool.wait_ge(s_kq, b - 1)
                pool.dma_start(qbc[:, b % 2, :], q_rows[b].partition_broadcast(P)).then_inc(s_qbc[b % 2], 16)

            diag_at = (0, 512, 1024, 896)

            def mask(buf):
                for n, at in enumerate(diag_at):
                    ins = pool.affine_select(out=buf[:, at:at + P], in_=buf[:, at:at + P], compare_op=ALU.is_gt,
                                             fill=0.0, base=0, pattern=[[1, P]], channel_multiplier=-1)
                return ins

            pool.wait_ge(s_pooled, 1)
            load_query(0)
            load_query(1)

            def mask_weights(h):
                pool.wait_ge(s_we, h + 1)
                mask(zs[:, h % 2, :]).then_inc(s_wm, 1)

            for h in range(SBH):
                pool.wait_ge(s_sp, h + 1)
                mask(ex[:, h % 2, :]).then_inc(s_spm, 1)
                if h:
                    mask_weights(h - 1)
                n = UNIT[("k", h)]
                unit_wait(pool, n)
                pool.wait_ge(s_qbc[h % 2], 16 * (h // 2 + 1))
                k_pages = unit(n).rearrange("p (g c) -> p g c", g=PAGES)
                pool.tensor_tensor(k_pages, k_pages, qbc[:, h % 2, :].unsqueeze(1).broadcast_to([P, PAGES, 512]),
                                   ALU.mult).then_inc(s_kq, 1)
                if h + 2 < TS:
                    load_query(h + 2)
            mask_weights(SBH - 1)

            for layer in range(2):
                routed = 2 * layer
                h_wait(pool, "wout" if layer == 0 else "woutc", KT - 1)
                pool.dma_start(wr[:, :, 0:NG], a["w_rg"][layer].rearrange("(k p) c -> p k c", p=P)).then_inc(s_rin, 16)
                pool.dma_start(wr[:, :, NG:20], a["w_re"][layer].rearrange("(k p) c -> p k c", p=P)).then_inc(s_rin, 16)
                pool.dma_start(br[:, 0:NG], a["b_rg"][layer].partition_broadcast(RT)).then_inc(s_rin, 16)
                pool.dma_start(br[:, NG:20], a["b_re"][layer].partition_broadcast(RT)).then_inc(s_rin, 16)
                kw = dict(channel_multiplier=0, allow_small_or_imprecise_dtypes=True)
                link(pool.iota(iot, [[1, CAP]], base=0, **kw))
                link(pool.iota(io16, [[1, NE]], base=0, **kw))
                link(pool.iota(prio, [[-1, NPG]], base=NPG, **kw))
                link(pool.iota(vals, [[T, 2], [RT, NRT]], base=1, channel_multiplier=1,
                               allow_small_or_imprecise_dtypes=True))
                pool.memset(xg, 0.0).then_inc(s_rc, 1)

                def gather(e, par):
                    pool.tensor_copy(idx[:, 0, par:par + 1], tab_i[:, 0, bass.ds(e * BLK, 1)]).then_inc(s_idx, 1)
                    wait_alone(s_idx, NE * layer + e + 1)
                    pool.indirect_dma_start(xg[:, par, :], None, x_rows[layer],
                                            bass.IndirectOffsetOnAxis(ap=idx[:, 0, par:par + 1], axis=0),
                                            bounds_check=last_token, oob_is_err=False).then_inc(s_xg[par], 16)

                def scatter(e, par):
                    pool.tensor_copy(idx[:, 1, par:par + 1], tab_i[:, 1, bass.ds(e * BLK, 1)]).then_inc(s_idy, 1)
                    wait_alone(s_idy, NE * layer + e + 1)
                    pool.indirect_dma_start(y_rows[layer],
                                            bass.IndirectOffsetOnAxis(ap=idx[:, 1, par:par + 1], axis=0),
                                            yo[:, par, :], None,
                                            bounds_check=last_result, oob_is_err=False).then_inc(s_ys[par], 16)

                pool.wait_ge(s_tab, routed + 1)
                for i in range(2):
                    pool.wait_ge(s_xr[i], 16 * ((3 if i == 0 else 2) * (layer + 1)))
                pool.wait_ge(s_rc, layer + 1)
                gather(0, 0)

                def expert_step(e0, j, last=False):
                    e = e0 + 2 * j
                    par = (e0 - 1) % 2
                    if not last:
                        pool.wait_ge(s_xtf, NE * layer + e)
                        gather(e + 1, par)
                    pool.wait_ge(s_y, NE * layer + e)
                    if e0 > 2 or not isinstance(j, int):
                        pool.wait_ge(s_ys[par], 16 * (NE // 2 * layer + (e0 - 1) // 2) + 16 * j)
                    scatter(e - 1, par)

                gather(1, 1)
                pool.wait_ge(s_xtf, NE * layer + 1)
                gather(2, 0)
                pool.wait_ge(s_y, NE * layer + 1)
                scatter(0, 0)
                with pool.Fori(0, 6) as j:
                    expert_step(2, j)
                    expert_step(3, j)
                expert_step(14, 0)
                expert_step(15, 0, last=True)
                pool.wait_ge(s_y, NE * layer + NE)
                pool.wait_ge(s_ys[1], 16 * (NE // 2 * layer + 7))
                scatter(15, 1)
                for i in range(2):
                    pool.wait_ge(s_ys[i], 16 * NE // 2 * (layer + 1))

                pool.wait_ge(s_tab, routed + 2)
                more = pool.value_load(flag[0:1, 0:1], min_val=0, max_val=1)
                o = ov[layer]
                with pool.If(more > 0):
                    with pool.Fori(0, NE) as e:
                        for r in range(1, BLK):
                            n = 4 * e + (r - 1)
                            pool.wait_ge(o["ys"], 16 * n)
                            pool.tensor_copy(idx[:, :, 0:1], tab_i[:, :, bass.ds(e * BLK + r, 1)]).then_inc(o["idx"], 1)
                            wait_alone(o["idx"], n + 1)
                            pool.indirect_dma_start(xg[:, 0, :], None, x_rows[layer],
                                                    bass.IndirectOffsetOnAxis(ap=idx[:, 0, 0:1], axis=0),
                                                    bounds_check=last_token, oob_is_err=False).then_inc(o["xg"], 16)
                            wait_alone(o["y"], n + 1)
                            pool.indirect_dma_start(y_rows[layer],
                                                    bass.IndirectOffsetOnAxis(ap=idx[:, 1, 0:1], axis=0),
                                                    yo[:, 0, :], None,
                                                    bounds_check=last_result, oob_is_err=False).then_inc(o["ys"], 16)
                    pool.wait_ge(o["ys"], 16 * 4 * NE)

                for i in range(NRT):
                    pool.dma_start(yg[:, i, :].rearrange("p (k d) -> p k d", k=2),
                                   y_rows[layer].rearrange("(k t) d -> t k d", k=2)[i * RT:(i + 1) * RT]
                                   ).then_inc(s_yg[i], 16)

                pool.wait_ge(s_filled, JOBS[("combine", (layer, KT - 1))][0] + 1)
                pool.dma_start(p_tok, a["p_prompt"][layer, 0].rearrange("(i p) c -> p i c", p=P)).then_inc(s_pin[0], 16)
                pool.dma_start(p_smp, a["p_sample"][layer, :, 0, :]).then_inc(s_pin[1], 16)

                if layer == 0:
                    h_wait(pool, "ple0", KT - 1)
                    pool.memset(cu[:, :, 0:CPAD], 0.0).then_inc(s_cuz, 1)
                    hs = a["state_conv"][0].rearrange("(g b) r c -> g (b r) c", g=2)
                    for g in range(2):
                        pool.dma_start(ch_rows[:, g, :], hs[g]).then_inc(s_cin, 16)
                    pool.wait_ge(s_drained["act"], JOBS[("csrow", 0)][2])
                    stored(pool.dma_start(out["conv_prompt"][0, 0], c_row))
                    stored(pool.dma_start(out["conv_sample"][0, :, CHIST - 1, :], cs_row))
                    pool.wait_ge(s_out, 16 * n_out[0])

            for i in range(5):
                pool.wait_ge(s_drained["act"], JOBS[("y", i)][2])
                if i < 4:
                    pool.dma_start(out["y_prompt"][0, i * P:(i + 1) * P, :], y_tok[:, i % 2, :]).then_inc(s_yt[i % 2], 16)
                else:
                    pool.dma_start(out["y_sample"][:, 0, :], y_tok[0:TS, i % 2, :]).then_inc(s_yt[i % 2], 16)
            pool.wait_ge(s_yt[0], 16 * 3)
            pool.wait_ge(s_yt[1], 16 * 2)

        @block.scalar
        def _(act):
            steps = [0]

            def link(ins):
                steps[0] += 1
                ins.then_inc(s_act, 1)
                act.wait_ge(s_act, steps[0])

            def copy_out(name, i, dst, src_of):
                s = drain_wait(act, name, i)
                nc.scalar.activation(dst, src_of(s), ACT.Copy).then_inc(s_drained["act"], 1)

            def halves(s):
                return s[:, :, 0:HALF]

            def norm(i, upd):
                before_it = 7 * (i + (i > 3))
                for k in range(KT):
                    h_wait(act, upd, k)
                    if k >= 2:
                        act.wait_ge(s_squsd, before_it + k - 1)
                    nc.scalar.activation(sq[:, k % 2, 0:T], hT[:, k, :], ACT.Square).then_inc(s_sq, 1)
                s = drain_wait(act, "norm", i)
                nc.scalar.activation(rms[:].rearrange("p (a b) -> p a b", a=2), halves(s), ACT.Sqrt,
                                     bias=eps[:], scale=MULT).then_inc(s_drained["act"], 1)

            act.wait_ge(s_const, 1)
            norm(0, "x")
            two = lambda t: t.rearrange("p (a b) -> p a b", a=2)
            for m in range(4):
                copy_out("q", m, two(qT[:, m, :]), halves)
            for i in range(2):
                copy_out("v", i, v_tok[:, 2 * i:2 * i + 2, :], lambda s: s)
            copy_out("v", 2, v_tok[0:TS, 4, :], lambda s: s[0:TS, 0, :])
            copy_out("qrow", 0, q_row, lambda s: s[0:TS, :, :])

            act.wait_ge(s_pooled, 1)
            act.wait_ge(s_stored, 1)
            z = ps_flat[:, 0:1280]

            def weights(h):
                act.wait_ge(s_dd, h + 1)
                nc.scalar.activation(zs[:, h % 2, :], zs[:, h % 2, :], ACT.Exp).then_inc(s_we, 1)

            for h in range(SBH):
                zb, eb = zs[:, h % 2, :], ex[:, h % 2, :]
                act.wait_ge(s_zf, h + 1)
                if h >= 2:
                    act.wait_ge(s_pv, h - 1)
                nc.scalar.activation(zb, z, ACT.Identity, bias=sbb[:, h:h + 1], scale=DH ** -0.5).then_inc(s_zs, 1)
                act.wait_ge(s_ab, h + 1)
                link(nc.scalar.activation(eb, eb, ACT.Exp))
                nc.scalar.activation(eb, eb, ACT.Ln, bias=one[:], scale=1.0).then_inc(s_ln, 1)
                if h:
                    weights(h - 1)
            weights(SBH - 1)
            flat = lambda t: t.rearrange("p b g h -> p (b g h)")
            act.wait_ge(s_za, 1)
            link(nc.scalar.activation(flat(zl), flat(zl), ACT.Exp))
            nc.scalar.activation(flat(zl), flat(zl), ACT.Ln, bias=one[:], scale=1.0).then_inc(s_zw, 1)
            act.wait_ge(s_za, 2)
            nc.scalar.activation(flat(zz), flat(zz), ACT.Exp).then_inc(s_zw, 1)

            norm(1, "wout")
            for layer in range(2):
                if layer:
                    norm(4, "woutc")
                for i in range(NRT):
                    s = drain_wait(act, "rows", (layer, i))
                    par = i % 2
                    seen = (3 if par == 0 else 2) * layer + i // 2
                    if seen:
                        act.wait_ge(s_xr[par], 16 * seen)
                    nc.scalar.activation(xr[:, par, :].rearrange("p (a b) -> p a b", a=2), s[0:RT, :, :],
                                         ACT.Copy).then_inc(s_drained["act"], 1)
                    act.wait_ge(s_drained["act"], JOBS[("rows", (layer, i))][2])
                    act.dma_start(x_rows[layer][i * RT:(i + 1) * RT, :], xr[:, par, :]).then_inc(s_xr[par], 16)
                for n in range(2):
                    act.wait_ge(s_ri, 2 * layer + n + 1)
                    v = rs[:, 0, :] if n == 0 else rs[:, 1, 0:NRT]
                    nc.scalar.activation(v, v, ACT.Exp).then_inc(s_ro, 1)

                def turn_tokens(e, base=NE * layer):
                    act.wait_ge(s_xtf, base + e + 1)
                    nc.scalar.activation(xgT, ps[:, 6:8, :].rearrange("p a (k c) -> p (a k) c", c=CAP),
                                         ACT.Copy).then_inc(s_xt, 1)

                def expert_step(e, last=False, base=NE * layer):
                    act.wait_ge(s_gf, base + e + 1)
                    act.wait_ge(s_hid, base + e)
                    nc.scalar.activation(sil, ps[:, 0, :], ACT.Silu).then_inc(s_sil, 1)
                    act.wait_ge(s_htf, base + e + 1)
                    nc.scalar.activation(hidT, ps[:, 4, :].rearrange("p (k c) -> p k c", c=CAP),
                                         ACT.Copy).then_inc(s_ht, 1)
                    if not last:
                        turn_tokens(e + 1)

                turn_tokens(0)
                expert_step(0)
                with act.Fori(0, 7) as j:
                    expert_step(2 * j + 1)
                    expert_step(2 * j + 2)
                expert_step(15, last=True)

                act.wait_ge(s_tab, 2 * layer + 2)
                more = act.value_load(flag[0:1, 0:1], min_val=0, max_val=1)
                o = ov[layer]
                with act.If(more > 0):
                    with act.Fori(0, NE) as e:
                        for r in range(4):
                            n = 4 * e + r
                            act.wait_ge(o["xtf"], n + 1)
                            nc.scalar.activation(xgT, ps[:, 6:8, :].rearrange("p a (k c) -> p (a k) c", c=CAP),
                                                 ACT.Copy).then_inc(o["xt"], 1)
                            act.wait_ge(o["guf"], n + 1)
                            nc.scalar.activation(sil, ps[:, 0, :], ACT.Silu).then_inc(o["sil"], 1)
                            act.wait_ge(o["htf"], n + 1)
                            nc.scalar.activation(hidT, ps[:, 4, :].rearrange("p (k c) -> p k c", c=CAP),
                                                 ACT.Copy).then_inc(o["ht"], 1)

                norm(2 if layer == 0 else 5, f"moe{layer}")
                s = drain_wait(act, "pT", (layer, 0))
                nc.scalar.activation(pT[:, :, 0:TP], s, ACT.Copy).then_inc(s_drained["act"], 1)
                s = drain_wait(act, "pT", (layer, 1))
                nc.scalar.activation(pT[:, :, TP:T], s[:, 0, 0:16].rearrange("p (k c) -> p k c", k=2),
                                     ACT.Copy).then_inc(s_drained["act"], 1)
                for m in range(KT):
                    s = drain_wait(act, "pgate", (layer, m))
                    if 8 * layer + m >= 2:
                        act.wait_ge(s_sig, 8 * layer + m - 1)
                    nc.scalar.activation(two(sig[:, m % 2, :]), halves(s), ACT.Sigmoid,
                                         bias=prm[:, B_PG + 8 * layer + m:B_PG + 8 * layer + m + 1]
                                         ).then_inc(s_drained["act"], 1)
                if layer:
                    break

                norm(3, "ple0")
                for m in range(KT):
                    s = drain_wait(act, "cg", m)
                    if m >= 2:
                        act.wait_ge(s_cu, m - 1)
                    nc.scalar.activation(two(csig[:, m % 2, :]), halves(s), ACT.Sigmoid).then_inc(s_drained["act"], 1)
                copy_out("crow", 0, two(c_row), lambda s: s[0:CHIST, :, :])
                copy_out("csrow", 0, two(cs_row), lambda s: s[0:TS, :, :])
                n = 0
                for m in range(CONV_DVE, KT):
                    for c in range(CW):
                        if n >= 4:
                            act.wait_ge(s_dused, n - 3)
                        nc.scalar.activation(diag[:, n % 4, :], ident[:], ACT.Copy,
                                             scale=wdw[:, m, c:c + 1]).then_inc(s_diag, 1)
                        n += 1
                    s = drain_wait(act, "conv", m)
                    nc.scalar.activation(acc[:, m, 0:TP], s[:, 0, :], ACT.Identity,
                                         bias=prm[:, B_DW + m:B_DW + m + 1], scale=1.0).then_inc(s_drained["act"], 1)
                s = drain_wait(act, "mean", 0)
                nc.scalar.activation(two(rms[:]), halves(s), ACT.Copy, scale=MULT).then_inc(s_drained["act"], 1)
                for k in range(KT):
                    act.wait_ge(s_xc, k + 1)
                    if k >= 2:
                        act.wait_ge(s_squsd, 7 * 4 + k - 1)
                    nc.scalar.activation(sq[:, k % 2, 0:T], acc[:, k, :], ACT.Square).then_inc(s_sq, 1)
                s = drain_wait(act, "var", 0)
                nc.scalar.activation(two(rms[:]), halves(s), ACT.Sqrt, bias=eps[:], scale=MULT).then_inc(s_drained["act"], 1)
                for k in range(KT):
                    act.wait_ge(s_lnx, k + 1)
                    nc.scalar.activation(xnT[:, k, :], acc[:, k, :], ACT.Silu, bias=prm[:, LN_B + k:LN_B + k + 1],
                                         scale=prm[:, LN_G + k:LN_G + k + 1]).then_inc(s_silu, 1)
            norm(6, "ple1")
            for i in range(5):
                if i >= 2:
                    act.wait_ge(s_yt[i % 2], 16 * (i // 2))
                n = P if i < 4 else TS
                copy_out("y", i, y_tok[0:n, i % 2, :].rearrange("p (a b) -> p a b", a=2), lambda s: s[0:n, :, :])

        @block.vector
        def _(dve):
            steps = [0]
            v = nc.vector

            def link(ins):
                steps[0] += 1
                ins.then_inc(s_dve, 1)
                dve.wait_ge(s_dve, steps[0])

            def halves(s):
                return s[:, :, 0:HALF]

            def two(t):
                return t.rearrange("p (a b) -> p a b", a=2)

            def norm(i, upd, gain):
                dve.wait_ge(s_drained["act"], JOBS[("norm", i)][2])
                link(v.reciprocal(rstd[:], rms[:]))
                for k in range(KT):
                    h_wait(dve, upd, k)
                    v.scalar_tensor_tensor(xnT[:, k, :], hT[:, k, :], prm[:, gain + k:gain + k + 1], rstd[:],
                                           ALU.mult, ALU.mult).then_inc(s_xn, 1)

            for i in range(4):
                s = drain_wait(dve, "x", i)
                v.tensor_copy(hT[:, 2 * i:2 * i + 2, 0:TP], s).then_inc(s_drained["dve"], 1)
            s = drain_wait(dve, "x", 4)
            v.tensor_copy(prm[:], s[:, 1, 0:N_PRM])
            v.tensor_copy(wdw[:].rearrange("p k c -> p (k c)"), s[:, 1, 128:128 + KT * CW])
            v.tensor_copy(hT[:, :, TP:T], s[:, 0, 0:KT * TS].rearrange("p (k c) -> p k c", k=KT)
                          ).then_inc(s_drained["dve"], 1)
            dve.wait_ge(s_const, 1)
            for g, w in enumerate(PW):
                link(v.tensor_scalar(cfix[:, g, :], cfix[:, g, :], float(w), None, ALU.min))
            link(v.reciprocal(cfix[:], cfix[:]))
            for g, w in enumerate(PW):
                link(v.tensor_scalar(cfix[:, g, :], cfix[:, g, :], float(w), None, ALU.mult))
            norm(0, "x", G_MIX)

            for m in range(4):
                s = drain_wait(dve, "k", m)
                v.tensor_copy(two(kT[:, m, :]), halves(s)).then_inc(s_drained["dve"], 1)
            for m in range(4):
                s = drain_wait(dve, "u", m)
                v.tensor_copy(two(up[:, m, PAD:PAD + T]), halves(s)).then_inc(s_drained["dve"], 1)
            for i in range(3):
                s = drain_wait(dve, "krow", i)
                if i < 2:
                    v.tensor_copy(k_tok[:, 2 * i:2 * i + 2, :], s).then_inc(s_drained["dve"], 1)
                else:
                    v.tensor_copy(k_tok[0:TS, 4, :], s[0:TS, 0, :]).then_inc(s_drained["dve"], 1)
            s = drain_wait(dve, "urow", 0)
            dve.wait_ge(s_upz, 1)
            v.tensor_copy(u_row, s[0:HIST, 0, :])
            v.tensor_copy(hist[:, :, :, 0:HIST], s[:, 1, 0:480].rearrange("p (g b r) -> p g b r", g=4, b=TS)
                          ).then_inc(s_drained["dve"], 1)
            dve.wait_ge(s_drained["dve"], JOBS[("urow", 0)][2])

            for g, w in enumerate(PW):
                src, width = up[:, g, :], 1
                for level in range(g + 1):
                    dst = sq[:, level % 2, :]
                    at = 2 * width - 1
                    link(v.tensor_tensor(dst[:, at:528], src[:, at:528], src[:, at - width:528 - width], ALU.add))
                    src, width = dst, 2 * width
                link(v.tensor_tensor(src[:, PAD:PAD + 16], src[:, PAD:PAD + 16], cfix[:, g, :], ALU.mult))
                link(v.tensor_copy(hist[:, g, :, HIST], up[:, g, PAD + TP:PAD + T]))
                link(v.scalar_tensor_tensor(up[:, g, PAD:PAD + TP], src[:, PAD:PAD + TP], 1.0 / w,
                                            up[:, g, PAD:PAD + TP], ALU.mult, ALU.subtract))
                link(v.tensor_reduce(rstd[:, 8 * g:8 * g + 8], hist[:, g, :, HIST + 1 - w:], AX, ALU.add))
                link(v.scalar_tensor_tensor(up[:, g, PAD + TP:PAD + T], rstd[:, 8 * g:8 * g + 8], 1.0 / w,
                                            up[:, g, PAD + TP:PAD + T], ALU.mult, ALU.subtract))
            dve.sem_inc(s_pooled, 1)

            dve.wait_ge(s_stored, 1)
            cstick = ps_flat[:, 1536:1536 + 1280]

            def attend_front(h):
                zb, eb = zs[:, h % 2, :], ex[:, h % 2, :]
                dve.wait_ge(s_zs, h + 1)
                if h >= 2:
                    dve.wait_ge(s_cf, h - 1)
                v.scalar_tensor_tensor(eb, zb, -1.0, zb, ALU.mult, ALU.min).then_inc(s_ab, 1)
                dve.wait_ge(s_ln, h + 1)
                v.scalar_tensor_tensor(eb, zb, 0.0, eb, ALU.max, ALU.add).then_inc(s_sp, 1)

            def attend_back(h):
                zb = zs[:, h % 2, :]
                dve.wait_ge(s_cf, h + 1)
                v.tensor_tensor(zb, zb, cstick, ALU.subtract).then_inc(s_dd, 1)
                n = UNIT[("k", h)]
                dve.wait_ge(s_kq, h + 1)
                v.tensor_reduce(zz[:, h, :, :].rearrange("p g h -> p (g h)"),
                                unit(n).rearrange("p (g c) -> p g c", c=DH), AX, ALU.add).then_inc(s_kused, 1)

            def attend_out(p):
                dve.wait_ge(s_pv, 2 * p + 2)
                v.tensor_copy(xnT[:, p, 0:TP], ps[:, 6 + p % 2, :]).then_inc(s_ot, 1)

            attend_front(0)
            for h in range(SBH):
                if h + 1 < SBH:
                    attend_front(h + 1)
                attend_back(h)
                if h and h % 2 == 0:
                    attend_out(h // 2 - 1)
            attend_out(3)

            flat = lambda t: t.rearrange("p b g h -> p (b g h)")
            by_head = lambda t: t.rearrange("p b g h -> p (b g) h")
            dve.wait_ge(s_kused, TS)
            link(v.scalar_tensor_tensor(by_head(zz), by_head(zz), DH ** -0.5,
                                        sbb[:].unsqueeze(1).broadcast_to([P, TS * PAGES, SBH]), ALU.mult, ALU.add))
            v.scalar_tensor_tensor(flat(zl), flat(zz), -1.0, flat(zz), ALU.mult, ALU.min).then_inc(s_za, 1)
            dve.wait_ge(s_zw, 1)
            link(v.scalar_tensor_tensor(flat(zl), flat(zz), 0.0, flat(zl), ALU.max, ALU.add))
            link(v.memset(zr[:, :, PAGES - 1, :], 0.0))
            for g in range(PAGES - 2, -1, -1):
                link(v.tensor_tensor(zr[:, :, g, :], zr[:, :, g + 1, :], zl[:, :, g + 1, :], ALU.add))
            dve.sem_inc(s_zv, 1)
            s = drain_wait(dve, "cs", 0)
            v.tensor_tensor(flat(zz), flat(zz), s[:, 0, :], ALU.subtract).then_inc(s_drained["dve"], 1)
            dve.wait_ge(s_drained["dve"], JOBS[("cs", 0)][2])
            dve.sem_inc(s_za, 1)
            s = drain_wait(dve, "vs", 0)
            o = s[:, 0, 0:64].rearrange("p (j b c) -> p j b c", j=4, b=TS)
            v.tensor_copy(xnT[0:64, 0:4, TP:T], o[0:64, :, :, 0])
            v.tensor_copy(xnT[64:P, 0:4, TP:T], o[64:P, :, :, 1]).then_inc(s_drained["dve"], 1)
            for m in range(4):
                s = drain_wait(dve, "poolproj", m)
                v.tensor_scalar(two(xnT[:, 4 + m, :]), halves(s), prm[:, P_SC + m:P_SC + m + 1], None, ALU.mult
                                ).then_inc(s_drained["dve"], 1)

            def add_to_h(name, i, m):
                s = drain_wait(dve, name, i)
                v.tensor_tensor(two(hT[:, m, :]), two(hT[:, m, :]), halves(s), ALU.add).then_inc(s_drained["dve"], 1)

            for m in range(KT):
                add_to_h("wout", m, m)
            norm(1, "wout", G_FFN)

            for layer in range(2):
                if layer:
                    norm(4, "woutc", G_FFN + 8)
                dve.wait_ge(s_rin, 64 * (layer + 1))
                dve.wait_ge(s_rc, layer + 1)
                b4 = lambda t: t.unsqueeze(2).broadcast_to([RT, NRT, 4])
                s = drain_wait(dve, "logits", layer)
                v.tensor_tensor(lg, s[0:RT, 0, 0:100].rearrange("p (i c) -> p i c", c=20),
                                br.unsqueeze(1).broadcast_to([RT, NRT, 20]), ALU.add).then_inc(s_drained["dve"], 1)
                dve.wait_ge(s_drained["dve"], JOBS[("logits", layer)][2])
                gl = lg[:, :, 0:NG]
                r5 = lambda n: rs[:, n, 0:NRT]
                r20 = lambda n: rs[:, n, :].rearrange("p (i c) -> p i c", c=4)
                pr = prio.unsqueeze(1).broadcast_to([RT, NRT, 4])

                def first_max(x, top, hot, t):
                    link(v.tensor_reduce(top, x, AX, ALU.max))
                    link(v.tensor_tensor(t, x, b4(top), ALU.is_equal))
                    link(v.tensor_tensor(t, t, pr, ALU.mult))
                    link(v.tensor_reduce(r5(9), t, AX, ALU.max))
                    link(v.tensor_tensor(hot, t, b4(r5(9)), ALU.is_equal))

                first_max(gl, r5(2), r20(3), r20(4))
                v.tensor_tensor(r20(0), gl, b4(r5(2)), ALU.subtract).then_inc(s_ri, 1)
                goh = r20(3).unsqueeze(3).broadcast_to([RT, NRT, NG, NPG])
                for g in range(NG):
                    link(v.tensor_tensor(mt[:, :, g, :], lg[:, :, NG + 4 * g:NG + 4 * g + 4],
                                         b4(r20(3)[:, :, g]), ALU.mult))
                link(v.tensor_reduce(r20(5), mt.rearrange("p i g e -> p i e g"), AX, ALU.add))
                first_max(r20(5), r5(6), r20(7), r20(4))
                link(v.scalar_tensor_tensor(r20(8), r20(7), -3e38, r20(5), ALU.mult, ALU.add))
                first_max(r20(8), r5(10), r20(11), r20(4))
                v.tensor_tensor(rs[:, 1, 0:NRT], r5(10), r5(6), ALU.subtract).then_inc(s_ri, 1)
                for mk, hot in ((m1, r20(7)), (m2, r20(11))):
                    for g in range(NG):
                        link(v.tensor_tensor(mk[:, :, g, :], hot, b4(r20(3)[:, :, g]), ALU.mult))
                f16 = lambda t: t.rearrange("p i g e -> p i (g e)")
                v.tensor_tensor(cnt, f16(m1), f16(m2), ALU.add).then_inc(s_cnt, 1)
                s = drain_wait(dve, "rank", layer)
                rank = s[0:RT, 0, 0:80].rearrange("p (i c) -> p i c", c=NE)
                rk = lambda n: rs[:, n, 0:10].rearrange("p (k i) -> p k i", k=2)
                ten = lambda n: rs[:, n, 0:10]
                for k, mk in enumerate((m1, m2)):
                    link(v.tensor_tensor(f16(mt), f16(mk), rank, ALU.mult))
                    link(v.tensor_reduce(rk(12)[:, k, :], f16(mt), AX, ALU.add))
                    link(v.tensor_tensor(f16(mt), f16(mk), io16.unsqueeze(1).broadcast_to([RT, NRT, NE]), ALU.mult))
                    link(v.tensor_reduce(rk(13)[:, k, :], f16(mt), AX, ALU.add))
                dve.sem_inc(s_drained["dve"], 1)
                link(v.tensor_scalar(ten(14), ten(12), float(CAP), None, ALU.is_ge))
                for n in range(2, BLK):
                    link(v.scalar_tensor_tensor(ten(14), ten(12), float(n * CAP), ten(14), ALU.is_ge, ALU.add))
                link(v.scalar_tensor_tensor(ten(15), ten(14), -float(CAP), ten(12), ALU.mult, ALU.add))
                link(v.scalar_tensor_tensor(ten(16), ten(13), float(BLK), ten(14), ALU.mult, ALU.add))
                link(v.tensor_reduce(rs[:, 17, 0:1], ten(14), AX, ALU.add))
                vl = vals.rearrange("p k i -> p (k i)")
                for n in range(10):
                    v.tensor_scalar(sel_c[:, n, :], iot, ten(15)[:, n:n + 1], None, ALU.is_equal)
                    ins = v.tensor_scalar(sel_b[:, n, :], iot[:, 0:NE * BLK], ten(16)[:, n:n + 1],
                                          vl[:, n:n + 1], ALU.is_equal, ALU.mult)
                ins.then_inc(s_sel, 1)
                dve.wait_ge(s_ro, 2 * layer + 2)
                link(v.tensor_reduce(r5(18), r20(0), AX, ALU.add))
                link(v.reciprocal(r5(18), r5(18)))
                link(v.tensor_scalar(r5(19), rs[:, 1, 0:NRT], 1.0, None, ALU.add))
                link(v.reciprocal(r5(19), r5(19)))
                link(v.tensor_tensor(wts[:, 0, :], r5(18), r5(19), ALU.mult))
                link(v.tensor_tensor(wts[:, 1, :], wts[:, 0, :], rs[:, 1, 0:NRT], ALU.mult))
                s = drain_wait(dve, "table", layer)
                link(v.tensor_scalar(tabf[:, 0, :], s[:, 0, 0:80], 0.0, UNUSED, ALU.is_equal, ALU.mult))
                link(v.scalar_tensor_tensor(tabf[:, 1, :], s[:, 0, 0:80], -1.0, tabf[:, 0, :], ALU.add, ALU.add))
                link(v.tensor_scalar(tabf[:, 2, :], tabf[:, 1, :], float(T), -float(T), ALU.is_ge, ALU.mult))
                link(v.tensor_tensor(tabf[:, 0, :], tabf[:, 1, :], tabf[:, 2, :], ALU.add))
                link(v.tensor_scalar(rs[0:1, 20, 0:1], s[0:1, 1, 0:1], 0.5, None, ALU.is_ge))
                link(v.tensor_copy(flag[:], rs[0:1, 20, 0:1]))
                link(v.tensor_copy(tab_i[:, 0, :], tabf[:, 0, :]))
                link(v.tensor_copy(tab_i[:, 1, :], tabf[:, 1, :]))
                dve.sem_inc(s_drained["dve"], 1)
                dve.sem_inc(s_tab, 2)

                def result(e, par, j, base=NE * layer):
                    dve.wait_ge(s_df, base + e + 1)
                    dve.wait_ge(s_ys[par], 16 * ((NE // 2) * layer + j))
                    v.tensor_copy(yo[:, par, :].rearrange("p (a b) -> p a b", a=2), ps[:, 2:4, :]).then_inc(s_y, 1)

                def hidden(e, base=NE * layer):
                    dve.wait_ge(s_uf, base + e + 1)
                    dve.wait_ge(s_sil, base + e + 1)
                    v.tensor_tensor(hid, sil, ps[:, 1, :], ALU.mult).then_inc(s_hid, 1)

                hidden(0)
                with dve.Fori(0, 7) as j:
                    hidden(2 * j + 1)
                    result(2 * j, 0, j)
                    hidden(2 * j + 2)
                    result(2 * j + 1, 1, j)
                hidden(15)
                result(14, 0, 7)
                result(15, 1, 7)

                more = dve.value_load(flag[0:1, 0:1], min_val=0, max_val=1)
                o = ov[layer]
                with dve.If(more > 0):
                    with dve.Fori(0, NE) as e:
                        for r in range(4):
                            n = 4 * e + r
                            dve.wait_ge(o["sil"], n + 1)
                            v.tensor_tensor(hid, sil, ps[:, 1, :], ALU.mult).then_inc(o["hid"], 1)
                            dve.wait_ge(o["df"], n + 1)
                            v.tensor_copy(yo[:, 0, :].rearrange("p (a b) -> p a b", a=2), ps[:, 2:4, :]
                                          ).then_inc(o["y"], 1)

                for i in range(NRT):
                    dve.wait_ge(s_yg[i], 16 * (layer + 1))
                    link(v.tensor_scalar(yg[:, i, 0:D], yg[:, i, 0:D], wts[:, 0, i:i + 1], None, ALU.mult))
                    v.scalar_tensor_tensor(yg[:, i, 0:D], yg[:, i, D:2 * D], wts[:, 1, i:i + 1], yg[:, i, 0:D],
                                           ALU.mult, ALU.add).then_inc(s_yc, 1)
                for d in range(KT):
                    s = drain_wait(dve, "combine", (layer, d))
                    v.tensor_tensor(hT[:, d, 0:416], hT[:, d, 0:416], s[:, 0, 0:416], ALU.add)
                    v.tensor_tensor(hT[:, d, 416:T], hT[:, d, 416:T], s[:, 1, 0:RT], ALU.add
                                    ).then_inc(s_drained["dve"], 1)

                norm(2 if layer == 0 else 5, f"moe{layer}", G_PG + 8 * layer)
                for m in range(KT):
                    s = drain_wait(dve, "pvalue", (layer, m))
                    dve.wait_ge(s_drained["act"], JOBS[("pgate", (layer, m))][2])
                    v.tensor_tensor(two(gv[:, m % 2, :]), two(sig[:, m % 2, :]), halves(s), ALU.mult
                                    ).then_inc(s_drained["dve"], 1)
                    dve.wait_ge(s_drained["dve"], JOBS[("pvalue", (layer, m))][2])
                    dve.sem_inc(s_sig, 1)
                    v.tensor_tensor(hT[:, m, :], hT[:, m, :], gv[:, m % 2, :], ALU.add).then_inc(s_h, 1)
                if layer:
                    break

                norm(3, "ple0", G_MIX + 8)
                for i in range(2):
                    s = drain_wait(dve, "chist", i)
                    for k in range(4):
                        c3 = chs[:, 4 * i + k, :].rearrange("p (b r) -> p b r", b=TS)
                        ins = v.tensor_copy(c3[:, :, 0:CHIST],
                                            s[:, k // 2, 240 * (k % 2):240 * (k % 2) + 240].rearrange(
                                                "p (b r) -> p b r", b=TS))
                    ins.then_inc(s_drained["dve"], 1)
                dve.wait_ge(s_cuz, 1)
                for m in range(KT):
                    s = drain_wait(dve, "ca", m)
                    dve.wait_ge(s_drained["act"], JOBS[("cg", m)][2])
                    link(v.tensor_tensor(cu[:, m, CPAD:CPAD + HALF], csig[:, m % 2, 0:HALF], s[:, 0, 0:HALF], ALU.mult))
                    link(v.tensor_tensor(cu[:, m, CPAD + HALF:CPAD + TP], csig[:, m % 2, HALF:TP],
                                         s[:, 1, 0:TP - HALF], ALU.mult))
                    c3 = chs[:, m, :].rearrange("p (b r) -> p b r", b=TS)
                    v.tensor_tensor(c3[:, :, CHIST], csig[:, m % 2, TP:T], s[:, 1, TP - HALF:HALF], ALU.mult
                                    ).then_inc(s_drained["dve"], 1)
                    dve.wait_ge(s_drained["dve"], JOBS[("ca", m)][2])
                    dve.sem_inc(s_cu, 1)
                for m in range(KT):
                    link(v.tensor_tensor(cprod.rearrange("p (b r) -> p b r", b=TS),
                                         chs[:, m, :].rearrange("p (b r) -> p b r", b=TS),
                                         wdw[:, m, :].unsqueeze(1).broadcast_to([P, TS, CW]), ALU.mult))
                    link(v.tensor_reduce(acc[:, m, TP:T], cprod.rearrange("p (b r) -> p b r", b=TS), AX, ALU.add))
                    link(v.tensor_scalar(acc[:, m, TP:T], acc[:, m, TP:T], prm[:, B_DW + m:B_DW + m + 1], None, ALU.add))
                for m in range(CONV_DVE):
                    link(v.tensor_scalar(acc[:, m, 0:TP], cu[:, m, 0:TP], wdw[:, m, 0:1],
                                         prm[:, B_DW + m:B_DW + m + 1], ALU.mult, ALU.add))
                    for c in range(1, CW):
                        link(v.scalar_tensor_tensor(acc[:, m, 0:TP], cu[:, m, c:c + TP], wdw[:, m, c:c + 1],
                                                    acc[:, m, 0:TP], ALU.mult, ALU.add))
                dve.sem_inc(s_acc, 1)
                dve.wait_ge(s_drained["act"], JOBS[("mean", 0)][2])
                for k in range(KT):
                    v.tensor_tensor(acc[:, k, :], acc[:, k, :], rms[:], ALU.subtract).then_inc(s_xc, 1)
                dve.wait_ge(s_drained["act"], JOBS[("var", 0)][2])
                link(v.reciprocal(rstd[:], rms[:]))
                for k in range(KT):
                    v.tensor_tensor(acc[:, k, :], acc[:, k, :], rstd[:], ALU.mult).then_inc(s_lnx, 1)
                for m in range(KT):
                    add_to_h("woutc", m, m)
            norm(6, "ple1", G_FIN)

        @block.tensor
        def _(pe):
            mm = nc.tensor.matmul

            def tr(dst, src, n):
                return nc.tensor.transpose(dst, src, ident[0:n, 0:n])

            def filled(ins):
                ins.then_inc(s_filled, 1)

            xn_seen = [0]

            def xn_wait(k):
                pe.wait_ge(s_xn, 8 * xn_seen[0] + k + 1)

            sq_seen = [0]

            def square_sums(name, i):
                s = fill_wait(pe, name, i)
                for k in range(KT):
                    pe.wait_ge(s_sq, 8 * sq_seen[0] + k + 1)
                    for half in range(2):
                        ins = mm(s[:, half, 0:HALF], ones[:], sq[:, k % 2, half * HALF:(half + 1) * HALF],
                                 start=(k == 0), stop=(k == KT - 1))
                    ins.then_inc(s_squsd if k < KT - 1 else s_filled, 1)
                sq_seen[0] += 1

            def channels(name, i, w, n, src=xnT, wait=None):
                s = fill_wait(pe, name, i)
                for k in range(n):
                    if wait:
                        wait(k)
                    for half in range(2):
                        ins = mm(s[:, half, 0:HALF], w[:, k, :], src[:, k, half * HALF:(half + 1) * HALF],
                                 start=(k == 0), stop=(k == n - 1))
                filled(ins)

            pe.wait_ge(s_const, 1)
            pe.wait_ge(s_in, 32)
            for i in range(4):
                s = fill_wait(pe, "x", i)
                for k in range(2):
                    for t in range(4):
                        ins = tr(s[:, k, t * P:(t + 1) * P], x_tok[:, t, (2 * i + k) * P:(2 * i + k + 1) * P], P)
                filled(ins)
            s = fill_wait(pe, "x", 4)
            pe.wait_ge(s_in2, 16 * 12)
            for k in range(KT):
                tr(s[:, 0, k * TS:(k + 1) * TS], x_smp[:, k * P:(k + 1) * P], TS)
            tr(s[:, 1, 0:N_PRM], prm_rows, N_PRM)
            for k in range(KT):
                ins = tr(s[:, 1, 128 + k * CW:128 + (k + 1) * CW], dw_rows[:, k * P:(k + 1) * P], CW)
            filled(ins)

            square_sums("norm", 0)
            for name, c in (("q", 0), ("k", 1)):
                unit_wait(pe, c)
                for m in range(4):
                    channels(name, m, w_view(c)[:, :, m * P:(m + 1) * P], KT, wait=xn_wait)
            unit_wait(pe, 2)
            for i in range(3):
                s = fill_wait(pe, "v", i)
                for b in range(2 if i < 2 else 1):
                    t = 2 * i + b
                    rows = P if t < 4 else TS
                    for k in range(KT):
                        ins = mm(s[0:rows, b, :], xnT[:, k, t * P:t * P + rows], w_view(2)[:, k, :],
                                 start=(k == 0), stop=(k == KT - 1))
                filled(ins)
            unit_wait(pe, 3)
            for m in range(4):
                channels("u", m, w_view(3)[:, :, m * P:(m + 1) * P], KT)
            xn_seen[0] += 1

            s = fill_wait(pe, "qrow", 0)
            pe.wait_ge(s_drained["act"], JOBS[("q", 3)][2])
            pe.wait_ge(s_drained["dve"], JOBS[("u", 3)][2])
            for m in range(4):
                tr(s[0:TS, 0, m * P:(m + 1) * P], qT[:, m, TP:T], P)
                ins = tr(s[0:TS, 1, m * P:(m + 1) * P], up[:, m, PAD + TP:PAD + T], P)
            filled(ins)
            for i in range(3):
                s = fill_wait(pe, "krow", i)
                for b in range(2 if i < 2 else 1):
                    t = 2 * i + b
                    rows = P if t < 4 else TS
                    for m in range(4):
                        ins = tr(s[0:rows, b, m * P:(m + 1) * P], kT[:, m, t * P:t * P + rows], P)
                filled(ins)
            s = fill_wait(pe, "urow", 0)
            pe.wait_ge(s_hist, 16)
            for m in range(4):
                tr(s[0:HIST, 0, m * P:(m + 1) * P], up[:, m, PAD + TP - HIST:PAD + TP], P)
                ins = tr(s[:, 1, m * 120:(m + 1) * 120], hist_rows[:, m * P:(m + 1) * P], 120)
            filled(ins)

            all_drained(pe, "urow", 0)
            at = {0: 0, 1: 512, 3: 896, 2: 1024}
            z0, c0 = 0, 1536

            def scores(h):
                rows = slice(64 * (h % 2), 64 * (h % 2) + 64)
                if h:
                    pe.wait_ge(s_zs, h)
                for kb in range(4):
                    ins = mm(ps_flat[:, z0 + at[kb]:z0 + at[kb] + TP - kb * P],
                             kT[rows, h // 2, kb * P:(kb + 1) * P], qT[rows, h // 2, kb * P:TP],
                             start=True, stop=True)
                ins.then_inc(s_zf, 1)

            def sticks(h):
                pe.wait_ge(s_spm, h + 1)
                if h:
                    pe.wait_ge(s_dd, h)
                sp = ex[:, h % 2, :]
                for kb in range(4):
                    for src in range(kb, 4):
                        off = (src - kb) * P
                        width = TP - src * P
                        ins = mm(ps_flat[:, c0 + at[kb] + off:c0 + at[kb] + off + width],
                                 tri[:] if src == kb else ones[:], sp[:, at[src]:at[src] + width],
                                 start=(src == kb), stop=(src == 3), skip_group_check=True)
                ins.then_inc(s_cf, 1)

            def values(h):
                pe.wait_ge(s_wm, h + 1)
                if h >= 4 and h % 2 == 0:
                    pe.wait_ge(s_ot, h // 2 - 1)
                rows = slice(64 * (h % 2), 64 * (h % 2) + 64)
                for kb in range(4):
                    ins = mm(ps[rows, 6 + (h // 2) % 2, kb * P:TP], v_tok[:, kb, h * DH:(h + 1) * DH],
                             zs[:, h % 2, at[kb]:at[kb] + TP - kb * P], start=(kb == 0), stop=(kb == 3),
                             skip_group_check=True)
                ins.then_inc(s_pv, 1)

            scores(0)
            for h in range(SBH):
                if h + 1 < SBH:
                    scores(h + 1)
                sticks(h)
                if h:
                    values(h - 1)
            values(SBH - 1)

            pe.wait_ge(s_dd, SBH)
            pe.wait_ge(s_ot, 4)
            pe.wait_ge(s_zs, SBH)
            s = slot(JOBS[("cs", 0)][0])
            pe.wait_ge(s_zv, 1)
            mm(s[:, 0, :], tri[:], zl.rearrange("p b g h -> p (b g h)"), start=True, stop=False)
            filled(mm(s[:, 0, :], ones[:], zr.rearrange("p b g h -> p (b g h)"), start=False, stop=True))
            s = slot(JOBS[("vs", 0)][0])
            pe.wait_ge(s_zw, 2)
            for b in range(TS):
                n = UNIT[("v", b)]
                unit_wait(pe, n)
                pages = unit(n).rearrange("p (g c) -> p g c", g=PAGES)
                for j in range(4):
                    for g in range(PAGES):
                        ins = mm(s[:, 0, j * 16 + b * 2:j * 16 + b * 2 + 2], pages[:, g, j * P:(j + 1) * P],
                                 zz[:, b, g, 2 * j:2 * j + 2], start=(g == 0), stop=(g == PAGES - 1))
                ins.then_inc(s_vused, 1)
            pe.wait_ge(s_vused, TS)
            pe.sem_inc(s_filled, 1)

            pe.wait_ge(s_pooled, 1)
            for m in range(4):
                channels("poolproj", m, wpool[:, m:m + 1, :], 1, src=up[:, m:m + 1, PAD:PAD + T])
            for c in range(2):
                n = UNIT[("w_out_ab", c)]
                unit_wait(pe, n)
                for m in range(4):
                    channels("wout", 4 * c + m, w_view(n)[:, :, m * P:(m + 1) * P], KT,
                             wait=(lambda k: pe.wait_ge(s_drained["dve"], JOBS[("poolproj", 3)][2]) if k == 4 else
                                   pe.wait_ge(s_drained["dve"], JOBS[("vs", 0)][2])) if not c and not m else None)

            square_sums("norm", 1)
            for layer in range(2):
                if layer:
                    square_sums("norm", 4)
                s = fill_wait(pe, "logits", layer)
                pe.wait_ge(s_rin, 64 * (layer + 1))
                for i in range(NRT):
                    for k in range(KT):
                        xn_wait(k)
                        ins = mm(s[0:RT, 0, i * 20:(i + 1) * 20], xnT[:, k, i * RT:(i + 1) * RT], wr[:, k, :],
                                 start=(k == 0), stop=(k == KT - 1))
                filled(ins)
                xn_seen[0] += 1
                for i in range(NRT):
                    s = fill_wait(pe, "rows", (layer, i))
                    for k in range(KT):
                        ins = tr(s[0:RT, k // 4, (k % 4) * P:(k % 4 + 1) * P], xnT[:, k, i * RT:(i + 1) * RT], P)
                    filled(ins)
                s = fill_wait(pe, "rank", layer)
                pe.wait_ge(s_cnt, layer + 1)
                for i in range(NRT):
                    for src in range(i + 1):
                        ins = mm(s[0:RT, 0, i * NE:(i + 1) * NE],
                                 before[0:RT, 0:RT] if src == i else ones[0:RT, 0:RT], cnt[:, src, :],
                                 start=(src == 0), stop=(src == i))
                filled(ins)
                s = fill_wait(pe, "table", layer)
                pe.wait_ge(s_sel, layer + 1)
                for n in range(10):
                    mm(s[:, 0, 0:NE * BLK], sel_c[:, n, :], sel_b[:, n, :], start=(n == 0), stop=(n == 9))
                filled(mm(s[0:1, 1, 0:1], ones[0:RT, 0:1], rs[:, 17, 0:1], start=True, stop=True))

                all_drained(pe, "table", layer)
                u0 = FIRST_EXPERT[layer]

                def turn_tokens(e, par, j, base=NE * layer):
                    pe.wait_ge(s_xg[par], 16 * ((NE // 2) * layer + j + 1))
                    pe.wait_ge(s_xt, base + e)
                    for k in range(KT):
                        ins = tr(ps[:, 6 + k // 4, (k % 4) * P:(k % 4 + 1) * P], xg[:, par, k * P:(k + 1) * P], P)
                    ins.then_inc(s_xtf, 1)

                def gate_up(e, n, j, base=NE * layer):
                    pe.wait_ge(s_xt, base + e + 1)
                    pe.wait_ge(s_hid, base + e)
                    for b, done in ((0, s_gf), (1, s_uf)):
                        pe.wait_ge(s_wland[(n + b) % RING], 16 * landed_count(n + b) + 16 * j)
                        for k in range(KT):
                            ins = mm(ps[:, b, :], xgT[:, k, :], w_view(n + b)[:, k, :],
                                     start=(k == 0), stop=(k == KT - 1))
                        ins.then_inc(done, 1)

                def turn_hidden(e, base=NE * layer):
                    pe.wait_ge(s_hid, base + e + 1)
                    pe.wait_ge(s_ht, base + e)
                    for k in range(FT):
                        ins = tr(ps[:, 4, k * P:(k + 1) * P], hid[:, k * P:(k + 1) * P], P)
                    ins.then_inc(s_htf, 1)

                def down(e, n, j, base=NE * layer):
                    pe.wait_ge(s_ht, base + e + 1)
                    pe.wait_ge(s_y, base + e)
                    pe.wait_ge(s_wland[n % RING], 16 * landed_count(n) + 16 * j)
                    w = unit(n).rearrange("p (k c) -> p k c", k=FT)
                    for b in range(2):
                        for k in range(FT):
                            ins = mm(ps[:, 2 + b, :], hidT[:, k, :], w[:, k, b * 512:(b + 1) * 512],
                                     start=(k == 0), stop=(k == FT - 1))
                    ins.then_inc(s_df, 1)

                def expert_step(e0, j, last=False):
                    e = e0 + 2 * j
                    n = u0 + 3 * e0 - 1
                    gate_up(e, n, j)
                    down(e - 1, n + 2, j)
                    turn_hidden(e)
                    if not last:
                        turn_tokens(e + 1, (e0 + 1) % 2, (e0 + 1) // 2 + j)

                turn_tokens(0, 0, 0)
                gate_up(0, u0, 0)
                turn_hidden(0)
                turn_tokens(1, 1, 0)
                with pe.Fori(0, 7) as j:
                    expert_step(1, j)
                    expert_step(2, j)
                expert_step(15, 0, last=True)
                down(15, u0 + 47, 0)

                pe.wait_ge(s_tab, 2 * layer + 2)
                more = pe.value_load(flag[0:1, 0:1], min_val=0, max_val=1)
                o = ov[layer]
                with pe.If(more > 0):
                    pe.wait_ge(s_y, NE * (layer + 1))
                    with pe.Fori(0, NE) as e:
                        pe.wait_ge(o["land"], 48 * e + 48)
                        for r in range(4):
                            m = 4 * e + r
                            pe.wait_ge(o["xg"], 16 * m + 16)
                            for k in range(KT):
                                ins = tr(ps[:, 6 + k // 4, (k % 4) * P:(k % 4 + 1) * P], xg[:, 0, k * P:(k + 1) * P], P)
                            ins.then_inc(o["xtf"], 1)
                            pe.wait_ge(o["xt"], m + 1)
                            for b in range(2):
                                for k in range(KT):
                                    ins = mm(ps[:, b, :], xgT[:, k, :], w_view(b)[:, k, :],
                                             start=(k == 0), stop=(k == KT - 1))
                            ins.then_inc(o["guf"], 1)
                            pe.wait_ge(o["hid"], m + 1)
                            for k in range(FT):
                                ins = tr(ps[:, 4, k * P:(k + 1) * P], hid[:, k * P:(k + 1) * P], P)
                            ins.then_inc(o["htf"], 1)
                            pe.wait_ge(o["ht"], m + 1)
                            w = unit(2).rearrange("p (k c) -> p k c", k=FT)
                            for b in range(2):
                                for k in range(FT):
                                    ins = mm(ps[:, 2 + b, :], hidT[:, k, :], w[:, k, b * 512:(b + 1) * 512],
                                             start=(k == 0), stop=(k == FT - 1))
                            ins.then_inc(o["df"], 1)
                        pe.wait_ge(o["df"], 4 * e + 4)
                        pe.sem_inc(o["eused"], 1)
                    pe.wait_ge(o["y"], 4 * NE)

                for d in range(KT):
                    s = slot(JOBS[("combine", (layer, d))][0])
                    if d >= 4:
                        fill_wait(pe, "combine", (layer, d))
                    else:
                        pe.wait_ge(s_y, NE * (layer + 1))
                    for i in range(NRT):
                        if not d:
                            pe.wait_ge(s_yc, NRT * layer + i + 1)
                        ins = tr(s[:, i // 4, (i % 4) * RT:(i % 4 + 1) * RT], yg[:, i, d * P:(d + 1) * P], RT)
                    filled(ins)

                square_sums("norm", 2 if layer == 0 else 5)
                s = fill_wait(pe, "pT", (layer, 0))
                pe.wait_ge(s_pin[0], 16 * (layer + 1))
                for k in range(2):
                    for t in range(4):
                        ins = tr(s[:, k, t * P:(t + 1) * P], p_tok[:, t, k * P:(k + 1) * P], P)
                filled(ins)
                s = fill_wait(pe, "pT", (layer, 1))
                pe.wait_ge(s_pin[1], 16 * (layer + 1))
                for k in range(2):
                    ins = tr(s[:, 0, k * TS:(k + 1) * TS], p_smp[:, k * P:(k + 1) * P], TS)
                filled(ins)
                nv = UNIT[("w_ple", layer)]
                for m in range(KT):
                    n = UNIT[("w_pg", layer, m // 4)]
                    unit_wait(pe, n)
                    channels("pgate", (layer, m), w_view(n)[:, :, (m % 4) * P:(m % 4 + 1) * P], KT, wait=xn_wait)
                    unit_wait(pe, nv)
                    pe.wait_ge(s_drained["act"], JOBS[("pT", (layer, 1))][2])
                    channels("pvalue", (layer, m), ple_view(nv)[:, :, m * P:(m + 1) * P], 2, src=pT)
                xn_seen[0] += 1
                if layer:
                    break

                square_sums("norm", 3)
                pe.wait_ge(s_cin, 32)
                for i in range(2):
                    s = fill_wait(pe, "chist", i)
                    for k in range(4):
                        for g in range(2):
                            off = 240 * (k % 2) + 120 * g
                            ins = tr(s[:, k // 2, off:off + 120], ch_rows[:, g, (4 * i + k) * P:(4 * i + k + 1) * P], 120)
                    filled(ins)
                for m in range(KT):
                    na, ng = UNIT[("w_in_c", m // 4)], UNIT[("w_in_c", 2 + m // 4)]
                    unit_wait(pe, ng)
                    cols = slice((m % 4) * P, (m % 4 + 1) * P)
                    channels("cg", m, w_view(ng)[:, :, cols], KT, wait=xn_wait)
                    unit_wait(pe, na)
                    channels("ca", m, w_view(na)[:, :, cols], KT)
                xn_seen[0] += 1
                pe.wait_ge(s_cu, KT)
                s = fill_wait(pe, "crow", 0)
                for k in range(KT):
                    ins = tr(s[0:CHIST, k // 4, (k % 4) * P:(k % 4 + 1) * P], cu[:, k, TP:TP + CPAD], P)
                filled(ins)
                s = fill_wait(pe, "csrow", 0)
                for k in range(KT):
                    c3 = chs[:, k, :].rearrange("p (b r) -> p b r", b=TS)
                    ins = tr(s[0:TS, k // 4, (k % 4) * P:(k % 4 + 1) * P], c3[:, :, CHIST], P)
                filled(ins)
                n = 0
                for m in range(CONV_DVE, KT):
                    s = fill_wait(pe, "conv", m)
                    for c in range(CW):
                        pe.wait_ge(s_diag, n + 1)
                        mm(s[:, 0, :], diag[:, n % 4, :], cu[:, m, c:c + TP], start=(c == 0), stop=(c == CW - 1)
                           ).then_inc(s_dused, 1)
                        n += 1
                    pe.wait_ge(s_dused, n)
                    pe.sem_inc(s_filled, 1)
                s = fill_wait(pe, "mean", 0)
                pe.wait_ge(s_acc, 1)
                pe.wait_ge(s_drained["act"], JOBS[("conv", KT - 1)][2])
                for k in range(KT):
                    for half in range(2):
                        ins = mm(s[:, half, 0:HALF], ones[:], acc[:, k, half * HALF:(half + 1) * HALF],
                                 start=(k == 0), stop=(k == KT - 1))
                filled(ins)
                square_sums("var", 0)
                for c in range(2):
                    n = UNIT[("w_out_c", c)]
                    unit_wait(pe, n)
                    for m in range(4):
                        channels("woutc", 4 * c + m, w_view(n)[:, :, m * P:(m + 1) * P], KT,
                                 wait=lambda k: pe.wait_ge(s_silu, k + 1))

            square_sums("norm", 6)
            for i in range(5):
                s = fill_wait(pe, "y", i)
                rows = P if i < 4 else TS
                for k in range(KT):
                    xn_wait(k)
                    ins = tr(s[0:rows, k // 4, (k % 4) * P:(k % 4 + 1) * P], xnT[:, k, i * P:i * P + rows], P)
                filled(ins)


_INS = ['x_prompt', 'x_sample', 'p_prompt', 'p_sample', 'cache_k', 'cache_v', 'state_pool', 'state_conv', 'page_table',
        'norm_mix', 'norm_ffn', 'norm_final', 'w_in_ab', 'sb_bias', 'w_pool', 'pool_scale', 'w_out_ab', 'w_in_c',
        'w_dw', 'b_dw', 'ln_g_c', 'ln_b_c', 'w_out_c', 'w_rg', 'b_rg', 'w_re', 'b_re', 'w_gate_e', 'w_up_e',
        'w_down_e', 'w_ple', 'w_ple_gate', 'b_ple_gate', 'g_ple_gate']
_OUTS = [('y_prompt', (1, 512, 1024)), ('y_sample', (8, 1, 1024)), ('k_prompt', (1, 1, 512, 8, 64)),
         ('v_prompt', (1, 1, 512, 8, 64)), ('pool_prompt', (1, 1, 15, 512)), ('conv_prompt', (1, 1, 30, 1024)),
         ('k_sample', (1, 8, 1, 8, 64)), ('v_sample', (1, 8, 1, 8, 64)), ('pool_sample', (1, 8, 15, 512)),
         ('conv_sample', (1, 8, 30, 1024))]


def kernel(**inputs):
    import numpy as _np
    import concourse.bacc as _bacc
    from concourse import mybir as _mybir
    from concourse.bass_utils import run_bass_kernel_spmd as _run

    nc = _bacc.Bacc("TRN2", target_bir_lowering=False, num_devices=1)
    arrays, a, out = {}, {}, {}
    for name in _INS:
        x = _np.ascontiguousarray(inputs[name])
        arrays[f"in_{name}"] = x
        a[name] = nc.dram_tensor(f"in_{name}", x.shape, _mybir.dt.from_np(x.dtype), kind="ExternalInput").ap()
    for name, shape in _OUTS:
        out[name] = nc.dram_tensor(f"out_{name}", shape, _mybir.dt.float32, kind="ExternalOutput").ap()
    decoder_step(nc, a, out)
    r = _run(nc, [arrays], core_ids=[0])
    return tuple(r.results[0][f"out_{name}"] for name, _ in _OUTS)
```

```python
from contextlib import ExitStack

import concourse.bass as bass
from concourse import mybir

ALU = mybir.AluOpType
ACT = mybir.ActivationFunctionType
F32 = mybir.dt.float32
R32 = mybir.dt.float32r
I32 = mybir.dt.int32
AX = mybir.AxisListType.X

P = 128
D = 1024
KT = D // P
TP, TS = 512, 8
T = TP + TS
HALF = T // 2
RT, NRT = 104, 5
SBH, DH = 8, 64
PAGES, PAGE = 8, 128
KEYS = 8
PIECES = 4
SUB = PAGE // KEYS
N_PHYS = 80
DPOOL, PW = 512, (2, 4, 8, 16)
HIST = 15
CW, CHIST = 31, 30
NG, NPG = 4, 4
NE = NG * NPG
F = 512
FT = F // P
DPLE = 256
EPS = 1e-6
CAP = 128
BLK = 5
EXTRA = (2 * T - 1) // CAP
UNUSED = float(1 << 20)
RING = 6
HU = 2048
NHU = 6 * NE
PAD = 16
CPAD = 30
CONV_DVE = 4
MULT = 1.0 / D

G_MIX, G_FFN, G_FIN, B_DW, LN_G, LN_B, B_PG, G_PG, P_SC = 0, 16, 32, 40, 48, 56, 64, 80, 96
N_PRM = 100


def unit_plan():
    units = [("w_in_ab", c) for c in range(4)]
    units += [("k", b) for b in range(TS)] + [("v", b) for b in range(TS)]
    units += [("w_out_ab", c) for c in range(2)]
    first_expert = []
    for layer in range(2):
        if layer:
            units += [("w_in_c", c) for c in (0, 2, 1, 3)] + [("w_out_c", c) for c in range(2)]
        first_expert.append(len(units))
        units += [("gate", layer, 0), ("up", layer, 0)]
        for e in range(1, NE):
            units += [("gate", layer, e), ("up", layer, e), ("down", layer, e - 1)]
        units += [("down", layer, NE - 1)]
        units += [("w_ple", layer), ("w_pg", layer, 0), ("w_pg", layer, 1)]
    return units, first_expert


UNITS, FIRST_EXPERT = unit_plan()
UNIT = {u: n for n, u in enumerate(UNITS)}


def is_cache(u):
    return u[0] in "kv"


def landed_count(n):
    kind = is_cache(UNITS[n])
    return sum(is_cache(UNITS[m]) == kind for m in range(n % RING, n + 1, RING))


def dense_plan():
    order = [("x", i, "dve") for i in range(5)]

    def norm(i):
        order.append(("norm", i, "act"))

    def moe(layer):
        order.append(("logits", layer, "dve"))
        order.extend(("rows", (layer, i), "act") for i in range(NRT))
        order.append(("rank", layer, "dve"))
        order.append(("table", layer, "dve"))
        order.extend(("combine", (layer, d), "dve") for d in range(KT))

    def ple(layer):
        order.extend(("pT", (layer, i), "act") for i in range(2))
        for m in range(KT):
            order.append(("pgate", (layer, m), "act"))
            order.append(("pvalue", (layer, m), "dve"))

    norm(0)
    order += [("q", m, "act") for m in range(4)] + [("k", m, "dve") for m in range(4)]
    order += [("v", i, "act") for i in range(3)] + [("u", m, "dve") for m in range(4)]
    order += [("qrow", 0, "act")] + [("krow", i, "dve") for i in range(3)] + [("urow", 0, "dve")]
    order += [("cs", 0, "dve"), ("vs", 0, "dve")]
    order += [("poolproj", m, "dve") for m in range(4)] + [("wout", m, "dve") for m in range(KT)]
    norm(1)
    moe(0)
    norm(2)
    ple(0)
    norm(3)
    order += [("chist", i, "dve") for i in range(2)]
    for m in range(KT):
        order += [("cg", m, "act"), ("ca", m, "dve")]
    order += [("crow", 0, "act"), ("csrow", 0, "act")]
    order += [("conv", m, "act") for m in range(CONV_DVE, KT)]
    order += [("mean", 0, "act"), ("var", 0, "act")]
    order += [("woutc", m, "dve") for m in range(KT)]
    norm(4)
    moe(1)
    norm(5)
    ple(1)
    norm(6)
    order += [("y", i, "act") for i in range(5)]
    jobs, drains = {}, {"act": 0, "dve": 0}
    for n, (name, i, engine) in enumerate(order):
        drains[engine] += 1
        jobs[(name, i)] = (n, engine, drains[engine])
    return jobs


JOBS = dense_plan()
BY_NUMBER = sorted(JOBS.values())


def decoder_step(nc, a, out):
    with ExitStack() as ctx:
        def sb(name, shape, dt=F32):
            return ctx.enter_context(nc.sbuf_tensor(name, shape, dt))

        def sb_parts(name, shape):
            with nc.sbuf_tensor(name, shape, F32) as whole:
                pass
            parts = sb(name + "_parts", shape, R32)
            return whole, parts

        def sem(name):
            return ctx.enter_context(nc.semaphore(name))

        x_rows = [nc.dram_tensor(f"x_rows{i}", (T, D), F32, kind="Internal").ap() for i in range(2)]
        y_rows = [nc.dram_tensor(f"y_rows{i}", (2 * T, D), F32, kind="Internal").ap() for i in range(2)]
        q_rows = nc.dram_tensor("q_rows", (TS, 512), F32, kind="Internal").ap()

        ps = ctx.enter_context(nc.psum_tensor("ps", [P, 8, 512], F32))
        ps_flat = ps[:].rearrange("p a b -> p (a b)")

        def slot(n):
            return ps[:, 2 * (n % 4):2 * (n % 4) + 2, :]

        hT = sb("hT", [P, KT, T])
        xnT, xnT_r = sb_parts("xnT", [P, KT, T])
        slots = [sb_parts(f"ring{i}", [P, 4096]) for i in range(RING)]
        sq = sb("sq", [P, 2, 528])
        rms = sb("rms", [P, T])
        rstd = sb("rstd", [P, T])
        ident = sb("ident", [P, P])
        tri = sb("tri", [P, P])
        before = sb("before", [P, P])
        ones = sb("ones", [P, P])
        prm = sb("prm", [P, N_PRM])
        wdw = sb("wdw", [P, KT, CW])
        wpool = sb("wpool", [P, 4, P])
        eps = sb("eps", [P, 1])
        one = sb("one", [P, 1])
        sbb = sb("sbb", [P, SBH])
        cfix = sb("cfix", [P, 4, 16])
        tab_i = sb("tab_i", [P, 2, NE * BLK], I32)
        idx = sb("idx", [P, 2, 2], I32)
        flag = sb("flag", [1, 1], I32)
        extra = sb("extra", [1, 2, EXTRA], I32)
        wts = sb("wts", [RT, 2, NRT])
        page_of = sb("page_of", [P, TS], I32)
        part_of = sb("part_of", [P, 1], I32)
        cache_row = sb("cache_row", [P, TS], I32)
        after = sb("after", [P, P])
        arena, arena_r = sb_parts("arena", [P, 16100])

        def shaped(v, shape):
            if len(shape) == 2:
                v = v.rearrange("p (a b) -> p a b", a=shape[0])
            if len(shape) == 3:
                v = v.rearrange("p (a b c) -> p a b c", a=shape[0], b=shape[1])
            return v

        class Arena:
            def __init__(self, at=0):
                self.at = at

            def __call__(self, *shape, rows=P):
                size = 1
                for s in shape:
                    size *= s
                self.at += size
                assert self.at <= 16100, self.at
                v, self.parts = (shaped(t[0:rows, self.at - size:self.at], shape) for t in (arena, arena_r))
                return v

        ar = Arena()
        x_tok = ar(4, D)
        x_smp = ar(D, rows=TS)
        prm_rows = ar(P, rows=N_PRM)
        dw_rows = ar(D, rows=CW)
        ar = Arena()
        qT = ar(4, T)
        kT = ar(4, T)
        v_tok = ar(NRT, 512)
        up = ar(4, PAD + T)
        spans = ar.at
        zs = ar(2, 1280)
        ex = ar(2, 1280)
        qbc = ar(2, 512)
        zz = ar(TS, KEYS, SBH)
        zl = ar(TS, KEYS, SBH)
        zr = qbc.rearrange("p a (b f h) -> p (a b) f h", b=TS, f=KEYS)[:, 0:TS]
        vo = arena[0:SBH, spans:spans + TS * 512].rearrange("p (b c) -> p b c", b=TS)
        ar = Arena(spans)
        k_tok = ar(NRT, 512)
        q_row = ar(2, 512, rows=TS)
        u_row = ar(512, rows=HIST)
        hist_rows = ar(512, rows=TS * HIST)
        hist = ar(4, TS, HIST + 1)
        ar = Arena()
        xr = ar(2, D, rows=RT)
        sel_c = ar(10, CAP, rows=RT)
        sel_b = ar(10, NE * BLK, rows=RT)
        xg = ar(2, D)
        xgT = ar(KT, CAP)
        xgT_r = ar.parts
        sil = ar(F)
        hid = ar(F)
        hidT = ar(FT, CAP)
        hidT_r = ar.parts
        yo = ar(2, D)
        ar(KT, CAP)
        xgT_lo = ar.parts
        ar(FT, CAP)
        hidT_lo = ar.parts
        wr = ar(KT, 20)
        br = ar(20, rows=RT)
        lg = ar(NRT, 20, rows=RT)
        rs = ar(40, NRT * 4, rows=RT)
        m1 = ar(NRT, NG, NPG, rows=RT)
        m2 = ar(NRT, NG, NPG, rows=RT)
        mt = ar(NRT, NG, NPG, rows=RT)
        cnt = ar(NRT, NE, rows=RT)
        iot = ar(CAP, rows=RT)
        io16 = ar(NE, rows=RT)
        prio = ar(NPG, rows=RT)
        vals = ar(2, NRT, rows=RT)
        tabf = ar(3, NE * BLK)
        beyond = ar(2, NE, BLK - 1, rows=1)
        taken = ar(2, NE * (BLK - 1), rows=1)
        pick = ar(EXTRA, NE * (BLK - 1), rows=1)
        picked = ar(EXTRA, rows=1)
        high = [xnT_r[:].rearrange("p k t -> p (k t)")[:, q * HU:(q + 1) * HU] for q in range(2)]
        high += [arena_r[:, q * HU:(q + 1) * HU] for q in range(2)]
        ar = Arena()
        yg = ar(NRT, 2 * D, rows=RT)
        ar = Arena()
        p_tok = ar(4, DPLE)
        p_smp = ar(DPLE, rows=TS)
        pT = ar(2, T)
        sig = ar(2, T)
        gv = ar(2, T)
        ar = Arena()
        cu = ar(KT, CPAD + TP)
        chs = ar(KT, TS * CW)
        acc = ar(KT, T)
        ch_rows = ar(2, D, rows=120)
        diag = ar(4, P)
        csig = ar(2, T)
        c_row, cs_row = ch_rows[0:CHIST, 0, :], ch_rows[0:TS, 1, :]
        cprod = ar(TS * CW)
        ar = Arena()
        y_tok = ar(2, D)

        s_const = sem("s_const")
        s_in = sem("s_in")
        s_in2 = sem("s_in2")
        s_wland = [sem(f"s_wland{i}") for i in range(RING)]
        s_cland = [sem(f"s_cland{i}") for i in range(RING)]
        s_vused = sem("s_vused")
        s_kused = sem("s_kused")
        s_filled = sem("s_filled")
        s_drained = {"act": sem("s_drained_act"), "dve": sem("s_drained_dve")}
        s_dve = sem("s_dve")
        s_act = sem("s_act")
        s_pool = sem("s_pool")
        s_sq = sem("s_sq")
        s_squsd = sem("s_squsd")
        s_xn = sem("s_xn")
        s_h = sem("s_h")
        s_out = sem("s_out")
        n_out = [0]

        s_pt = sem("s_pt")
        s_qrow = sem("s_qrow")
        s_qbc = [sem(f"s_qbc{i}") for i in range(2)]
        s_kq = sem("s_kq")
        s_hist, s_upz, s_cuz = sem("s_hist"), sem("s_upz"), sem("s_cuz")
        s_stored = sem("s_stored")
        s_zf, s_zs, s_ab, s_ln = sem("s_zf"), sem("s_zs"), sem("s_ab"), sem("s_ln")
        s_sp, s_spm, s_cf, s_dd = sem("s_sp"), sem("s_spm"), sem("s_cf"), sem("s_dd")
        s_we, s_wm, s_pv, s_ot = sem("s_we"), sem("s_wm"), sem("s_pv"), sem("s_ot")
        s_zv, s_za, s_zw, s_vo = sem("s_zv"), sem("s_za"), sem("s_zw"), sem("s_vo")
        s_part, s_rows = sem("s_part"), sem("s_rows")
        s_pooled, s_opool = sem("s_pooled"), sem("s_opool")
        s_rin = sem("s_rin")
        s_rc = sem("s_rc")
        s_cnt, s_sel, s_tab = sem("s_cnt"), sem("s_sel"), sem("s_tab")
        s_ri, s_ro = sem("s_ri"), sem("s_ro")
        s_xr = [sem(f"s_xr{i}") for i in range(2)]
        s_xg = [sem(f"s_xg{i}") for i in range(2)]
        s_idx, s_idy = sem("s_idx"), sem("s_idy")
        s_xtf, s_xt = sem("s_xtf"), sem("s_xt")
        s_sil, s_hid, s_htf, s_ht, s_y = sem("s_sil"), sem("s_hid"), sem("s_htf"), sem("s_ht"), sem("s_y")
        s_hi, s_lo, s_hused = sem("s_hi"), sem("s_lo"), sem("s_hused")
        s_xtl, s_htl = sem("s_xtl"), sem("s_htl")
        s_ys = [sem(f"s_ys{i}") for i in range(2)]
        s_yg = [sem(f"s_yg{i}") for i in range(NRT)]
        s_yc = sem("s_yc")
        ov = [{k: sem(f"s_ov{layer}_{k}") for k in
               ("land", "eused", "spdone", "idx", "xg", "xtf", "xt", "guf", "sil", "hid", "htf", "ht", "df", "y", "ys")}
              for layer in range(2)]
        s_pin = [sem(f"s_pin{i}") for i in range(2)]
        s_pT, s_sig = sem("s_pT"), sem("s_sig")
        s_cin, s_chs = sem("s_cin"), sem("s_chs")
        s_csig, s_cu = sem("s_csig"), sem("s_cu")
        s_crow = sem("s_crow")
        s_diag, s_dused = sem("s_diag"), sem("s_dused")
        s_acc, s_xc, s_lnx, s_silu = sem("s_acc"), sem("s_xc"), sem("s_lnx"), sem("s_silu")
        s_yt = [sem(f"s_yt{i}") for i in range(2)]
        s_cvf = sem("s_cvf")

        def unit(n):
            return slots[n % RING][0][:]

        def w_view(n):
            return unit(n).rearrange("p (k c) -> p k c", k=KT)

        def fill_wait(pe, name, i):
            n = JOBS[(name, i)][0]
            if n >= 4:
                _, engine, count = BY_NUMBER[n - 4]
                pe.wait_ge(s_drained[engine], count)
            return slot(n)

        def drain_wait(eng, name, i):
            n = JOBS[(name, i)][0]
            eng.wait_ge(s_filled, n + 1)
            return slot(n)

        def all_drained(pe, name, i):
            upto = JOBS[(name, i)][0]
            for engine in ("act", "dve"):
                counts = [c for n, e, c in BY_NUMBER[: upto + 1] if e == engine]
                pe.wait_ge(s_drained[engine], counts[-1])

        def unit_wait(eng, n):
            if is_cache(UNITS[n]):
                eng.wait_ge(s_cland[n % RING], 16 * landed_count(n))
            else:
                eng.wait_ge(s_wland[n % RING], 16 * landed_count(n))

        def h_wait(eng, upd, k):
            if upd == "x":
                eng.wait_ge(s_drained["dve"], JOBS[("x", 4)][2])
            elif upd[:3] == "ple":
                eng.wait_ge(s_h, 8 * int(upd[3]) + k + 1)
            else:
                job = ("combine", (int(upd[3]), k)) if upd[:3] == "moe" else (upd, k)
                eng.wait_ge(s_drained["dve"], JOBS[job][2])

        def half_units(kind, layer, e):
            if isinstance(e, int) and e == 0 and kind != "down":
                return NHU * layer + (2 if kind == "gate" else 4)
            if isinstance(e, int) and e == NE - 1 and kind == "down":
                return NHU * (layer + 1)
            return NHU * layer + 6 * e + {"gate": 0, "up": 2, "down": 10}[kind]

        def used_wait(eng, n):
            u = UNITS[n]
            if u[0] == "k":
                eng.wait_ge(s_kused, u[1] + 1)
            elif u[0] == "v":
                eng.wait_ge(s_vused, u[1] + 1)
            elif u[0] in ("gate", "up", "down"):
                eng.wait_ge(s_hused, half_units(*u))
            else:
                last = {"w_in_ab": lambda c: ("qkvu"[c], 2 if c == 2 else 3), "w_out_ab": lambda c: ("wout", 4 * c + 3),
                        "w_in_c": lambda c: ("ca", 4 * (c % 2) + 3), "w_out_c": lambda c: ("woutc", 4 * c + 3),
                        "w_ple": lambda layer: ("pvalue", (layer, KT - 1)),
                        "w_pg": lambda layer, c: ("pgate", (layer, 4 * c + 3))}[u[0]](*u[1:])
                eng.wait_ge(s_filled, JOBS[last][0] + 1)

        def stored(ins):
            n_out[0] += 1
            ins.then_inc(s_out, 16)

        def unit_source(u):
            if u[0] in ("w_in_ab", "w_out_ab", "w_in_c", "w_out_c"):
                return a[u[0]][0].rearrange("(k p) c -> p k c", p=P)[:, :, u[1] * 512:(u[1] + 1) * 512]
            if u[0] == "w_ple":
                return a["w_ple"][u[1]].rearrange("(k p) c -> p k c", p=P)
            return a["w_ple_gate"][u[1]].rearrange("(k p) c -> p k c", p=P)[:, :, u[2] * 512:(u[2] + 1) * 512]

        def ple_view(n):
            return unit(n)[:, 0:2048].rearrange("p (k c) -> p k c", k=2)

        block = ctx.enter_context(nc.Block())

        @block.sync
        def _(sp):
            def free_wait(n):
                if n >= RING:
                    used_wait(sp, n - RING)

            def load(n):
                free_wait(n)
                src = unit_source(UNITS[n])
                dst = ple_view(n) if UNITS[n][0] == "w_ple" else w_view(n)
                sp.dma_start(dst, src).then_inc(s_wland[n % RING], 16)

            for g in range(PAGES):
                sp.dma_start(page_of[SUB * g:SUB * g + SUB, :], a["page_table"][:, g].partition_broadcast(SUB),
                             allow_slow_non_contiguous=True).then_inc(s_pt, 16)
            sp.dma_start(x_tok, a["x_prompt"][0].rearrange("(i p) d -> p i d", p=P)).then_inc(s_in, 16)
            sp.dma_start(x_smp, a["x_sample"][:, 0, :]).then_inc(s_in, 16)
            load(0)
            sp.wait_ge(s_in2, 16 * 12)
            for n in range(1, 4):
                load(n)
            load(UNIT[("w_out_ab", 0)])
            load(UNIT[("w_out_ab", 1)])

            for layer in range(2):
                if layer:
                    for u in (("w_in_c", 0), ("w_in_c", 2), ("w_in_c", 1), ("w_in_c", 3),
                              ("w_out_c", 0), ("w_out_c", 1)):
                        load(UNIT[u])
                u0 = FIRST_EXPERT[layer]
                gate, upw, down = (a[w][layer].rearrange("e (k p) c -> p (e k) c", p=P)
                                   for w in ("w_gate_e", "w_up_e", "w_down_e"))

                def expert_part(w, e, s):
                    k = w.shape[1] // NE
                    return slots[s][0][:].rearrange("p (k c) -> p k c", k=k), w[:, bass.ds(e * k, k), :]

                def expert_load(n, w, e):
                    sp.dma_start(*expert_part(w, e, n % RING)).then_inc(s_wland[n % RING], 16)

                def load_step(e):
                    n = u0 + 3 * e - 1
                    for i, (w, x) in enumerate(((gate, e), (upw, e), (down, e - 1))):
                        free_wait(n + i)
                        expert_load(n + i, w, x)

                def load_step_in_loop(e0, e):
                    n = u0 + 3 * e0 - 1
                    for i, (w, x, kind) in enumerate(((gate, e, "gate"), (upw, e, "up"), (down, e - 1, "down"))):
                        sp.wait_ge(s_hused, half_units(kind, layer, x - 2))
                        expert_load(n + i, w, x)

                for n, w in ((u0, gate), (u0 + 1, upw)):
                    free_wait(n)
                    expert_load(n, w, 0)
                load_step(1)
                load_step(2)
                with sp.Fori(0, 6) as j:
                    load_step_in_loop(3, 2 * j + 3)
                    load_step_in_loop(4, 2 * j + 4)
                load_step(15)
                free_wait(u0 + 47)
                expert_load(u0 + 47, down, 15)

                sp.wait_ge(s_tab, 2 * layer + 2)
                more = sp.value_load(flag[0:1, 0:1], min_val=0, max_val=1)
                with sp.If(more > 0):
                    with sp.Fori(0, EXTRA) as n:
                        column = sp.value_load(extra[0:1, 0, bass.ds(n, 1)], min_val=0, max_val=NE * BLK - 1)
                        with sp.If(column > 0):
                            e = sp.value_load(extra[0:1, 1, bass.ds(n, 1)], min_val=0, max_val=NE - 1)
                            sp.wait_ge(ov[layer]["eused"], n + 1)
                            for s, w in enumerate((gate, upw, down)):
                                sp.dma_start(*expert_part(w, e, s)).then_inc(ov[layer]["land"], 16)
                            sp.wait_ge(ov[layer]["eused"], n + 2)
                            sp.sem_inc(ov[layer]["spdone"], 1)
                for u in (("w_ple", layer), ("w_pg", layer, 0), ("w_pg", layer, 1)):
                    load(UNIT[u])

        @block.gpsimd
        def _(pool):
            steps = [0]
            last_token, last_result = pool.to_reg(T - 1), pool.to_reg(2 * T - 1)
            last_cache_row = pool.to_reg(N_PHYS * SUB - 1)

            def wait_alone(semaphore, count):
                if not isinstance(count, int):
                    count = pool.to_reg(count)
                pool.wait_ge(s_const, 1)
                pool.wait_ge(semaphore, count)

            def link(ins):
                steps[0] += 1
                ins.then_inc(s_pool, 1)
                pool.wait_ge(s_pool, steps[0])

            pool.iota(part_of[:], [[0, 1]], base=0, channel_multiplier=1).then_inc(s_part, 1)
            link(pool.memset(ones[:], 1.0))
            link(pool.memset(ident[:], 0.0))
            link(pool.affine_select(out=ident[:], in_=ident[:], compare_op=ALU.not_equal, fill=1.0, base=0,
                                    pattern=[[-1, P]], channel_multiplier=1))
            link(pool.affine_select(out=tri[:], in_=ones[:], compare_op=ALU.is_ge, fill=0.0, base=0,
                                    pattern=[[-1, P]], channel_multiplier=1))
            link(pool.affine_select(out=before[:], in_=ones[:], compare_op=ALU.is_gt, fill=0.0, base=0,
                                    pattern=[[1, P]], channel_multiplier=-1))
            link(pool.affine_select(out=after[:], in_=ones[:], compare_op=ALU.is_gt, fill=0.0, base=0,
                                    pattern=[[-1, P]], channel_multiplier=1))
            link(pool.memset(eps[:], EPS))
            link(pool.memset(one[:], 1.0))
            link(pool.iota(cfix[:], [[0, 4], [1, 16]], base=1, channel_multiplier=0,
                           allow_small_or_imprecise_dtypes=True))
            pool.memset(idx[:], 0).then_inc(s_const, 1)

            cache = {kind: a[f"cache_{kind}"][0].rearrange("n (s f) h d -> (n s) (f h d)", f=KEYS) for kind in "kv"}

            def load_cache(kind, b):
                n = UNIT[(kind, b)]
                if n >= RING:
                    used_wait(pool, n - RING)
                pool.indirect_dma_start(unit(n), None, cache[kind],
                                        bass.IndirectOffsetOnAxis(ap=cache_row[:, b:b + 1], axis=0),
                                        bounds_check=last_cache_row, oob_is_err=False).then_inc(s_cland[n % RING], 16)

            pool.wait_ge(s_rows, 1)
            load_cache("k", 0)
            load_cache("k", 1)

            stored(pool.dma_start(out["pool_sample"][0, :, 0:HIST - 1, :], a["state_pool"][0, :, 1:HIST, :]))
            stored(pool.dma_start(out["conv_sample"][0, :, 0:CHIST - 1, :], a["state_conv"][0, :, 1:CHIST, :]))

            pool.wait_ge(s_filled, JOBS[("x", 4)][0] + 1)
            pool.memset(up[:, :, 0:PAD], 0.0).then_inc(s_upz, 1)
            pool.dma_start(hist_rows, a["state_pool"][0].rearrange("b r c -> (b r) c")).then_inc(s_hist, 16)

            for b in range(2, 6):
                load_cache("k", b)

            pool.wait_ge(s_drained["act"], JOBS[("qrow", 0)][2])
            pool.dma_start(q_rows, q_row[:, 0, :]).then_inc(s_qrow, 16)
            stored(pool.dma_start(out["pool_sample"][0, :, HIST - 1, :], q_row[:, 1, :]))
            stored(pool.dma_start(out["v_prompt"][0, 0].rearrange("(i p) h d -> p i (h d)", p=P), v_tok[:, 0:4, :]))
            stored(pool.dma_start(out["v_sample"][0, :, 0].rearrange("b h d -> b (h d)"), v_tok[0:TS, 4, :]))
            pool.wait_ge(s_drained["dve"], JOBS[("krow", 2)][2])
            stored(pool.dma_start(out["k_prompt"][0, 0].rearrange("(i p) h d -> p i (h d)", p=P), k_tok[:, 0:4, :]))
            stored(pool.dma_start(out["k_sample"][0, :, 0].rearrange("b h d -> b (h d)"), k_tok[0:TS, 4, :]))
            pool.wait_ge(s_drained["dve"], JOBS[("urow", 0)][2])
            stored(pool.dma_start(out["pool_prompt"][0, 0], u_row))
            pool.wait_ge(s_out, 16 * n_out[0])
            pool.wait_ge(s_qrow, 16)
            pool.sem_inc(s_stored, 1)

            def load_query(b):
                if b >= 2:
                    pool.wait_ge(s_kq, PIECES * (b - 1))
                pool.dma_start(qbc[:, b % 2, :], q_rows[b].partition_broadcast(P)).then_inc(s_qbc[b % 2], 16)

            diag_at = (0, 512, 1024, 896)

            def mask(buf):
                for n, at in enumerate(diag_at):
                    ins = pool.affine_select(out=buf[:, at:at + P], in_=buf[:, at:at + P], compare_op=ALU.is_gt,
                                             fill=0.0, base=0, pattern=[[1, P]], channel_multiplier=-1)
                return ins

            pool.wait_ge(s_pooled, 1)
            load_query(0)
            load_query(1)

            def mask_weights(h):
                pool.wait_ge(s_we, h + 1)
                mask(zs[:, h % 2, :]).then_inc(s_wm, 1)

            for h in range(SBH):
                if h:
                    mask_weights(h - 1)
                pool.wait_ge(s_sp, h + 1)
                mask(ex[:, h % 2, :]).then_inc(s_spm, 1)
                n = UNIT[("k", h)]
                unit_wait(pool, n)
                pool.wait_ge(s_qbc[h % 2], 16 * (h // 2 + 1))
                for piece in range(PIECES):
                    width = KEYS // PIECES
                    keys = unit(n).rearrange("p (f c) -> p f c", f=KEYS)[:, piece * width:(piece + 1) * width, :]
                    pool.tensor_tensor(keys, keys, qbc[:, h % 2, :].unsqueeze(1).broadcast_to([P, width, 512]),
                                       ALU.mult).then_inc(s_kq, 1)
                if h + 2 < TS:
                    load_query(h + 2)
                if h >= 2:
                    load_cache(*(("k", h + 4) if h < 4 else ("v", h - 4)))
            mask_weights(SBH - 1)
            for b in range(4, TS):
                load_cache("v", b)

            for layer in range(2):
                routed = 2 * layer
                h_wait(pool, "wout" if layer == 0 else "woutc", KT - 1)
                pool.dma_start(wr[:, :, 0:NG], a["w_rg"][layer].rearrange("(k p) c -> p k c", p=P)).then_inc(s_rin, 16)
                pool.dma_start(wr[:, :, NG:20], a["w_re"][layer].rearrange("(k p) c -> p k c", p=P)).then_inc(s_rin, 16)
                pool.dma_start(br[:, 0:NG], a["b_rg"][layer].partition_broadcast(RT)).then_inc(s_rin, 16)
                pool.dma_start(br[:, NG:20], a["b_re"][layer].partition_broadcast(RT)).then_inc(s_rin, 16)
                kw = dict(channel_multiplier=0, allow_small_or_imprecise_dtypes=True)
                link(pool.iota(iot, [[1, CAP]], base=0, **kw))
                link(pool.iota(io16, [[1, NE]], base=0, **kw))
                link(pool.iota(prio, [[-1, NPG]], base=NPG, **kw))
                link(pool.iota(vals, [[T, 2], [RT, NRT]], base=1, channel_multiplier=1,
                               allow_small_or_imprecise_dtypes=True))
                for k, pattern, base in ((0, [[BLK, NE], [1, BLK - 1]], 1), (1, [[1, NE], [0, BLK - 1]], 0)):
                    link(pool.iota(beyond[:, k, :, :], pattern, base=base, **kw))
                pool.memset(xg, 0.0).then_inc(s_rc, 1)

                def gather(e, par):
                    pool.tensor_copy(idx[:, 0, par:par + 1], tab_i[:, 0, bass.ds(e * BLK, 1)]).then_inc(s_idx, 1)
                    wait_alone(s_idx, NE * layer + e + 1)
                    pool.indirect_dma_start(xg[:, par, :], None, x_rows[layer],
                                            bass.IndirectOffsetOnAxis(ap=idx[:, 0, par:par + 1], axis=0),
                                            bounds_check=last_token, oob_is_err=False).then_inc(s_xg[par], 16)

                def scatter(e, par):
                    pool.tensor_copy(idx[:, 1, par:par + 1], tab_i[:, 1, bass.ds(e * BLK, 1)]).then_inc(s_idy, 1)
                    wait_alone(s_idy, NE * layer + e + 1)
                    pool.indirect_dma_start(y_rows[layer],
                                            bass.IndirectOffsetOnAxis(ap=idx[:, 1, par:par + 1], axis=0),
                                            yo[:, par, :], None,
                                            bounds_check=last_result, oob_is_err=False).then_inc(s_ys[par], 16)

                pool.wait_ge(s_tab, routed + 1)
                for i in range(2):
                    pool.wait_ge(s_xr[i], 16 * ((3 if i == 0 else 2) * (layer + 1)))
                pool.wait_ge(s_rc, layer + 1)
                gather(0, 0)

                def expert_step(e0, j, last=False):
                    e = e0 + 2 * j
                    par = (e0 - 1) % 2
                    if not last:
                        pool.wait_ge(s_xtf, NE * layer + e)
                        gather(e + 1, par)
                    pool.wait_ge(s_y, NE * layer + e)
                    if e0 > 2 or not isinstance(j, int):
                        pool.wait_ge(s_ys[par], 16 * (NE // 2 * layer + (e0 - 1) // 2) + 16 * j)
                    scatter(e - 1, par)

                gather(1, 1)
                pool.wait_ge(s_xtf, NE * layer + 1)
                gather(2, 0)
                pool.wait_ge(s_y, NE * layer + 1)
                scatter(0, 0)
                expert_step(2, 0)
                expert_step(3, 0)
                with pool.Fori(0, 5) as j:
                    expert_step(4, j)
                    expert_step(5, j)
                expert_step(14, 0)
                expert_step(15, 0, last=True)
                pool.wait_ge(s_y, NE * layer + NE)
                pool.wait_ge(s_ys[1], 16 * (NE // 2 * layer + 7))
                scatter(15, 1)
                for i in range(2):
                    pool.wait_ge(s_ys[i], 16 * NE // 2 * (layer + 1))

                pool.wait_ge(s_tab, routed + 2)
                more = pool.value_load(flag[0:1, 0:1], min_val=0, max_val=1)
                o = ov[layer]
                with pool.If(more > 0):
                    with pool.Fori(0, EXTRA) as n:
                        column = pool.value_load(extra[0:1, 0, bass.ds(n, 1)], min_val=0, max_val=NE * BLK - 1)
                        with pool.If(column > 0):
                            pool.tensor_copy(idx[:, :, 0:1], tab_i[:, :, bass.ds(column, 1)]).then_inc(o["idx"], 1)
                            wait_alone(o["idx"], n + 1)
                            pool.indirect_dma_start(xg[:, 0, :], None, x_rows[layer],
                                                    bass.IndirectOffsetOnAxis(ap=idx[:, 0, 0:1], axis=0),
                                                    bounds_check=last_token, oob_is_err=False).then_inc(o["xg"], 16)
                            wait_alone(o["y"], n + 1)
                            pool.indirect_dma_start(y_rows[layer],
                                                    bass.IndirectOffsetOnAxis(ap=idx[:, 1, 0:1], axis=0),
                                                    yo[:, 0, :], None,
                                                    bounds_check=last_result, oob_is_err=False).then_inc(o["ys"], 16)
                            pool.wait_ge(o["ys"], 16 * n + 16)

                for i in range(NRT):
                    pool.dma_start(yg[:, i, :].rearrange("p (k d) -> p k d", k=2),
                                   y_rows[layer].rearrange("(k t) d -> t k d", k=2)[i * RT:(i + 1) * RT]
                                   ).then_inc(s_yg[i], 16)

                pool.wait_ge(s_filled, JOBS[("combine", (layer, KT - 1))][0] + 1)
                pool.dma_start(p_tok, a["p_prompt"][layer, 0].rearrange("(i p) c -> p i c", p=P)).then_inc(s_pin[0], 16)
                pool.dma_start(p_smp, a["p_sample"][layer, :, 0, :]).then_inc(s_pin[1], 16)

                if layer == 0:
                    h_wait(pool, "ple0", KT - 1)
                    pool.memset(cu[:, :, 0:CPAD], 0.0).then_inc(s_cuz, 1)
                    hs = a["state_conv"][0].rearrange("(g b) r c -> g (b r) c", g=2)
                    for g in range(2):
                        pool.dma_start(ch_rows[:, g, :], hs[g]).then_inc(s_cin, 16)
                    pool.wait_ge(s_drained["act"], JOBS[("csrow", 0)][2])
                    stored(pool.dma_start(out["conv_prompt"][0, 0], c_row))
                    stored(pool.dma_start(out["conv_sample"][0, :, CHIST - 1, :], cs_row))
                    pool.wait_ge(s_out, 16 * n_out[0])

            for i in range(5):
                pool.wait_ge(s_drained["act"], JOBS[("y", i)][2])
                if i < 4:
                    pool.dma_start(out["y_prompt"][0, i * P:(i + 1) * P, :], y_tok[:, i % 2, :]).then_inc(s_yt[i % 2], 16)
                else:
                    pool.dma_start(out["y_sample"][:, 0, :], y_tok[0:TS, i % 2, :]).then_inc(s_yt[i % 2], 16)
            pool.wait_ge(s_yt[0], 16 * 3)
            pool.wait_ge(s_yt[1], 16 * 2)

        @block.scalar
        def _(act):
            steps = [0]

            def link(ins):
                steps[0] += 1
                ins.then_inc(s_act, 1)
                act.wait_ge(s_act, steps[0])

            for name, row in (("norm_mix", G_MIX), ("norm_ffn", G_FFN), ("b_ple_gate", B_PG), ("g_ple_gate", G_PG)):
                act.dma_start(prm_rows[row:row + 16, :], a[name].rearrange("l (k p) -> (l k) p", p=P)).then_inc(s_in2, 16)
            act.dma_start(prm_rows[G_FIN:G_FIN + 8, :], a["norm_final"].rearrange("(k p) -> k p", p=P)).then_inc(s_in2, 16)
            for name, row, n in (("b_dw", B_DW, 8), ("ln_g_c", LN_G, 8), ("ln_b_c", LN_B, 8), ("pool_scale", P_SC, 4)):
                act.dma_start(prm_rows[row:row + n, :], a[name][0].rearrange("(k p) -> k p", p=P)).then_inc(s_in2, 16)
            act.dma_start(dw_rows, a["w_dw"][0]).then_inc(s_in2, 16)
            act.dma_start(sbb[:], a["sb_bias"][0].partition_broadcast(P)).then_inc(s_in2, 16)
            act.dma_start(wpool[:], a["w_pool"][0].rearrange("g c d -> c g d")).then_inc(s_in2, 16)

            def copy_out(name, i, dst, src_of):
                s = drain_wait(act, name, i)
                nc.scalar.activation(dst, src_of(s), ACT.Copy).then_inc(s_drained["act"], 1)

            def halves(s):
                return s[:, :, 0:HALF]

            def norm(i, upd):
                before_it = 7 * (i + (i > 3))
                for k in range(KT):
                    h_wait(act, upd, k)
                    if k >= 2:
                        act.wait_ge(s_squsd, before_it + k - 1)
                    nc.scalar.activation(sq[:, k % 2, 0:T], hT[:, k, :], ACT.Square).then_inc(s_sq, 1)
                s = drain_wait(act, "norm", i)
                nc.scalar.activation(rms[:].rearrange("p (a b) -> p a b", a=2), halves(s), ACT.Sqrt,
                                     bias=eps[:], scale=MULT).then_inc(s_drained["act"], 1)

            act.wait_ge(s_const, 1)
            norm(0, "x")
            two = lambda t: t.rearrange("p (a b) -> p a b", a=2)
            for m in range(4):
                copy_out("q", m, two(qT[:, m, :]), halves)
            for i in range(2):
                copy_out("v", i, v_tok[:, 2 * i:2 * i + 2, :], lambda s: s)
            copy_out("v", 2, v_tok[0:TS, 4, :], lambda s: s[0:TS, 0, :])
            copy_out("qrow", 0, q_row, lambda s: s[0:TS, :, :])

            act.wait_ge(s_pooled, 1)
            act.wait_ge(s_stored, 1)
            act.preload_act_table_set("natural_log_exp_and_others")
            z = ps_flat[:, 0:1280]

            def weights(h):
                act.wait_ge(s_dd, h + 1)
                nc.scalar.activation(zs[:, h % 2, :], zs[:, h % 2, :], ACT.Exp).then_inc(s_we, 1)

            for h in range(SBH):
                zb, eb = zs[:, h % 2, :], ex[:, h % 2, :]
                act.wait_ge(s_zf, h + 1)
                if h >= 2:
                    act.wait_ge(s_pv, h - 1)
                nc.scalar.activation(zb, z, ACT.Identity, bias=sbb[:, h:h + 1], scale=DH ** -0.5).then_inc(s_zs, 1)
                act.wait_ge(s_ab, h + 1)
                link(nc.scalar.activation(eb, eb, ACT.Exp))
                nc.scalar.activation(eb, eb, ACT.Ln, bias=one[:], scale=1.0).then_inc(s_ln, 1)
                if h:
                    weights(h - 1)
            weights(SBH - 1)
            flat = lambda t: t.rearrange("p b g h -> p (b g h)")
            act.wait_ge(s_za, 1)
            link(nc.scalar.activation(flat(zl), flat(zl), ACT.Exp))
            nc.scalar.activation(flat(zl), flat(zl), ACT.Ln, bias=one[:], scale=1.0).then_inc(s_zw, 1)
            act.wait_ge(s_za, 2)
            nc.scalar.activation(flat(zz), flat(zz), ACT.Exp).then_inc(s_zw, 1)

            norm(1, "wout")
            for layer in range(2):
                if layer:
                    norm(4, "woutc")
                for i in range(NRT):
                    s = drain_wait(act, "rows", (layer, i))
                    par = i % 2
                    seen = (3 if par == 0 else 2) * layer + i // 2
                    if seen:
                        act.wait_ge(s_xr[par], 16 * seen)
                    nc.scalar.activation(xr[:, par, :].rearrange("p (a b) -> p a b", a=2), s[0:RT, :, :],
                                         ACT.Copy).then_inc(s_drained["act"], 1)
                    act.wait_ge(s_drained["act"], JOBS[("rows", (layer, i))][2])
                    act.dma_start(x_rows[layer][i * RT:(i + 1) * RT, :], xr[:, par, :]).then_inc(s_xr[par], 16)
                for n in range(2):
                    act.wait_ge(s_ri, 2 * layer + n + 1)
                    v = rs[:, 0, :] if n == 0 else rs[:, 1, 0:NRT]
                    nc.scalar.activation(v, v, ACT.Exp).then_inc(s_ro, 1)

                u0 = FIRST_EXPERT[layer]

                def high_part(hu0, j, free=True):
                    if free:
                        act.wait_ge(s_hused, NHU * layer + hu0 - 3 + 12 * j)
                    n = u0 + hu0 // 2
                    if hu0 % 2 == 0:
                        act.wait_ge(s_wland[n % RING], 16 * landed_count(n) + 16 * j)
                    at = HU * (hu0 % 2)
                    nc.scalar.activation(high[hu0 % 4], unit(n)[:, at:at + HU], ACT.Copy).then_inc(s_hi, 1)

                def turn_tokens(e, base=NE * layer):
                    act.wait_ge(s_xtf, base + e + 1)
                    nc.scalar.activation(xgT_r, ps[:, 6:8, :].rearrange("p a (k c) -> p (a k) c", c=CAP),
                                         ACT.Copy).then_inc(s_xt, 1)

                def result(e, par, j, base=NE * layer):
                    act.wait_ge(s_hused, half_units("down", layer, e))
                    if not isinstance(j, int) or layer or j:
                        act.wait_ge(s_ys[par], 16 * ((NE // 2) * layer + j))
                    nc.scalar.activation(yo[:, par, :].rearrange("p (a b) -> p a b", a=2), ps[:, 2:4, :], ACT.Copy
                                         ).then_inc(s_y, 1)

                def expert_step(e0, j, last=False, base=NE * layer):
                    e, h = e0 + 2 * j, 6 * e0 + 2 if e0 else 4
                    high_part(h, j)
                    high_part(h + 1, j)
                    act.wait_ge(s_hused, half_units("gate", layer, e))
                    if not isinstance(e, int) or base + e:
                        act.wait_ge(s_hid, base + e)
                    nc.scalar.activation(sil, ps[:, 0, :], ACT.Silu).then_inc(s_sil, 1)
                    high_part(h + 2, j)
                    high_part(h + 3, j)
                    if not last:
                        turn_tokens(e + 1)
                        if e0:
                            high_part(h + 4, j)
                            high_part(h + 5, j)
                    if e0:
                        result(e - 1, (e0 - 1) % 2, (e0 - 1) // 2 + j)
                    act.wait_ge(s_htf, base + e + 1)
                    nc.scalar.activation(hidT_r, ps[:, 4, :].rearrange("p (k c) -> p k c", c=CAP),
                                         ACT.Copy).then_inc(s_ht, 1)

                act.wait_ge(s_filled, JOBS[("rows", (layer, NRT - 1))][0] + 1)
                high_part(0, 0, free=False)
                high_part(1, 0, free=False)
                act.wait_ge(s_filled, JOBS[("table", layer)][0] + 1)
                for i in range(2):
                    act.wait_ge(s_xr[i], 16 * ((3 if i == 0 else 2) * (layer + 1)))
                high_part(2, 0, free=False)
                high_part(3, 0, free=False)
                turn_tokens(0)
                expert_step(0, 0)
                expert_step(1, 0)
                expert_step(2, 0)
                with act.Fori(0, 6) as j:
                    expert_step(3, j)
                    expert_step(4, j)
                expert_step(15, 0, last=True)
                result(15, 1, 7)

                act.wait_ge(s_tab, 2 * layer + 2)
                more = act.value_load(flag[0:1, 0:1], min_val=0, max_val=1)
                o = ov[layer]
                with act.If(more > 0):
                    with act.Fori(0, EXTRA) as n:
                        column = act.value_load(extra[0:1, 0, bass.ds(n, 1)], min_val=0, max_val=NE * BLK - 1)
                        with act.If(column > 0):
                            act.wait_ge(o["xtf"], n + 1)
                            nc.scalar.activation(xgT, ps[:, 6:8, :].rearrange("p a (k c) -> p (a k) c", c=CAP),
                                                 ACT.Copy).then_inc(o["xt"], 1)
                            act.wait_ge(o["guf"], n + 1)
                            nc.scalar.activation(sil, ps[:, 0, :], ACT.Silu).then_inc(o["sil"], 1)
                            act.wait_ge(o["htf"], n + 1)
                            nc.scalar.activation(hidT, ps[:, 4, :].rearrange("p (k c) -> p k c", c=CAP),
                                                 ACT.Copy).then_inc(o["ht"], 1)

                norm(2 if layer == 0 else 5, f"moe{layer}")
                s = drain_wait(act, "pT", (layer, 0))
                nc.scalar.activation(pT[:, :, 0:TP], s, ACT.Copy).then_inc(s_drained["act"], 1)
                s = drain_wait(act, "pT", (layer, 1))
                nc.scalar.activation(pT[:, :, TP:T], s[:, 0, 0:16].rearrange("p (k c) -> p k c", k=2),
                                     ACT.Copy).then_inc(s_drained["act"], 1)
                for m in range(KT):
                    s = drain_wait(act, "pgate", (layer, m))
                    if 8 * layer + m >= 2:
                        act.wait_ge(s_sig, 8 * layer + m - 1)
                    nc.scalar.activation(two(sig[:, m % 2, :]), halves(s), ACT.Sigmoid,
                                         bias=prm[:, B_PG + 8 * layer + m:B_PG + 8 * layer + m + 1]
                                         ).then_inc(s_drained["act"], 1)
                if layer:
                    break

                norm(3, "ple0")
                for m in range(KT):
                    s = drain_wait(act, "cg", m)
                    if m >= 2:
                        act.wait_ge(s_cu, m - 1)
                    nc.scalar.activation(two(csig[:, m % 2, :]), halves(s), ACT.Sigmoid).then_inc(s_drained["act"], 1)
                copy_out("crow", 0, two(c_row), lambda s: s[0:CHIST, :, :])
                copy_out("csrow", 0, two(cs_row), lambda s: s[0:TS, :, :])
                n = 0
                for m in range(CONV_DVE, KT):
                    for c in range(CW):
                        if n >= 4:
                            act.wait_ge(s_dused, n - 3)
                        nc.scalar.activation(diag[:, n % 4, :], ident[:], ACT.Copy,
                                             scale=wdw[:, m, c:c + 1]).then_inc(s_diag, 1)
                        n += 1
                    s = drain_wait(act, "conv", m)
                    nc.scalar.activation(acc[:, m, 0:TP], s[:, 0, :], ACT.Identity,
                                         bias=prm[:, B_DW + m:B_DW + m + 1], scale=1.0).then_inc(s_drained["act"], 1)
                s = drain_wait(act, "mean", 0)
                nc.scalar.activation(two(rms[:]), halves(s), ACT.Copy, scale=MULT).then_inc(s_drained["act"], 1)
                for k in range(KT):
                    act.wait_ge(s_xc, k + 1)
                    if k >= 2:
                        act.wait_ge(s_squsd, 7 * 4 + k - 1)
                    nc.scalar.activation(sq[:, k % 2, 0:T], acc[:, k, :], ACT.Square).then_inc(s_sq, 1)
                s = drain_wait(act, "var", 0)
                nc.scalar.activation(two(rms[:]), halves(s), ACT.Sqrt, bias=eps[:], scale=MULT).then_inc(s_drained["act"], 1)
                for k in range(KT):
                    act.wait_ge(s_lnx, k + 1)
                    nc.scalar.activation(xnT[:, k, :], acc[:, k, :], ACT.Silu, bias=prm[:, LN_B + k:LN_B + k + 1],
                                         scale=prm[:, LN_G + k:LN_G + k + 1]).then_inc(s_silu, 1)
            norm(6, "ple1")
            for i in range(5):
                if i >= 2:
                    act.wait_ge(s_yt[i % 2], 16 * (i // 2))
                n = P if i < 4 else TS
                copy_out("y", i, y_tok[0:n, i % 2, :].rearrange("p (a b) -> p a b", a=2), lambda s: s[0:n, :, :])

        @block.vector
        def _(dve):
            steps = [0]
            v = nc.vector

            def link(ins):
                steps[0] += 1
                ins.then_inc(s_dve, 1)
                dve.wait_ge(s_dve, steps[0])

            def halves(s):
                return s[:, :, 0:HALF]

            def two(t):
                return t.rearrange("p (a b) -> p a b", a=2)

            def norm(i, upd, gain):
                dve.wait_ge(s_drained["act"], JOBS[("norm", i)][2])
                link(v.reciprocal(rstd[:], rms[:]))
                for k in range(KT):
                    h_wait(dve, upd, k)
                    v.scalar_tensor_tensor(xnT[:, k, :], hT[:, k, :], prm[:, gain + k:gain + k + 1], rstd[:],
                                           ALU.mult, ALU.mult).then_inc(s_xn, 1)

            dve.wait_ge(s_part, 1)
            link(v.tensor_scalar(part_of[:], part_of[:], SUB - 1, None, ALU.bitwise_and))
            dve.wait_ge(s_pt, 16 * PAGES)
            link(v.tensor_scalar(cache_row[:], page_of[:], SUB.bit_length() - 1, None, ALU.logical_shift_left))
            v.tensor_tensor(cache_row[:], cache_row[:], part_of[:].broadcast_to([P, TS]), ALU.add).then_inc(s_rows, 1)

            for i in range(4):
                s = drain_wait(dve, "x", i)
                v.tensor_copy(hT[:, 2 * i:2 * i + 2, 0:TP], s).then_inc(s_drained["dve"], 1)
            s = drain_wait(dve, "x", 4)
            v.tensor_copy(prm[:], s[:, 1, 0:N_PRM])
            v.tensor_copy(wdw[:].rearrange("p k c -> p (k c)"), s[:, 1, 128:128 + KT * CW])
            v.tensor_copy(hT[:, :, TP:T], s[:, 0, 0:KT * TS].rearrange("p (k c) -> p k c", k=KT)
                          ).then_inc(s_drained["dve"], 1)
            dve.wait_ge(s_const, 1)
            for g, w in enumerate(PW):
                link(v.tensor_scalar(cfix[:, g, :], cfix[:, g, :], float(w), None, ALU.min))
            link(v.reciprocal(cfix[:], cfix[:]))
            for g, w in enumerate(PW):
                link(v.tensor_scalar(cfix[:, g, :], cfix[:, g, :], float(w), None, ALU.mult))
            norm(0, "x", G_MIX)

            for m in range(4):
                s = drain_wait(dve, "k", m)
                v.tensor_copy(two(kT[:, m, :]), halves(s)).then_inc(s_drained["dve"], 1)
            for m in range(4):
                s = drain_wait(dve, "u", m)
                v.tensor_copy(two(up[:, m, PAD:PAD + T]), halves(s)).then_inc(s_drained["dve"], 1)
            for i in range(3):
                s = drain_wait(dve, "krow", i)
                if i < 2:
                    v.tensor_copy(k_tok[:, 2 * i:2 * i + 2, :], s).then_inc(s_drained["dve"], 1)
                else:
                    v.tensor_copy(k_tok[0:TS, 4, :], s[0:TS, 0, :]).then_inc(s_drained["dve"], 1)
            s = drain_wait(dve, "urow", 0)
            dve.wait_ge(s_upz, 1)
            v.tensor_copy(u_row, s[0:HIST, 0, :])
            v.tensor_copy(hist[:, :, :, 0:HIST], s[:, 1, 0:480].rearrange("p (g b r) -> p g b r", g=4, b=TS)
                          ).then_inc(s_drained["dve"], 1)
            dve.wait_ge(s_drained["dve"], JOBS[("urow", 0)][2])

            for g, w in enumerate(PW):
                src, width = up[:, g, :], 1
                for level in range(g + 1):
                    dst = sq[:, level % 2, :]
                    at = 2 * width - 1
                    link(v.tensor_tensor(dst[:, at:528], src[:, at:528], src[:, at - width:528 - width], ALU.add))
                    src, width = dst, 2 * width
                link(v.tensor_tensor(src[:, PAD:PAD + 16], src[:, PAD:PAD + 16], cfix[:, g, :], ALU.mult))
                link(v.tensor_copy(hist[:, g, :, HIST], up[:, g, PAD + TP:PAD + T]))
                link(v.scalar_tensor_tensor(up[:, g, PAD:PAD + TP], src[:, PAD:PAD + TP], 1.0 / w,
                                            up[:, g, PAD:PAD + TP], ALU.mult, ALU.subtract))
                link(v.tensor_reduce(rstd[:, 8 * g:8 * g + 8], hist[:, g, :, HIST + 1 - w:], AX, ALU.add))
                link(v.scalar_tensor_tensor(up[:, g, PAD + TP:PAD + T], rstd[:, 8 * g:8 * g + 8], 1.0 / w,
                                            up[:, g, PAD + TP:PAD + T], ALU.mult, ALU.subtract))
            dve.sem_inc(s_pooled, 1)

            dve.wait_ge(s_stored, 1)
            cstick = ps_flat[:, 1536:1536 + 1280]

            def sum_keys(b):
                n = UNIT[("k", b)]
                dve.wait_ge(s_kq, PIECES * (b + 1))
                v.tensor_reduce(zz[:, b, :, :].rearrange("p f h -> p (f h)"),
                                unit(n).rearrange("p (f c) -> p f c", c=DH), AX, ALU.add).then_inc(s_kused, 1)

            def attend_front(h):
                zb, eb = zs[:, h % 2, :], ex[:, h % 2, :]
                dve.wait_ge(s_zs, h + 1)
                if h >= 2:
                    dve.wait_ge(s_cf, h - 1)
                v.scalar_tensor_tensor(eb, zb, -1.0, zb, ALU.mult, ALU.min).then_inc(s_ab, 1)
                if h:
                    attend_back(h - 1)
                dve.wait_ge(s_ln, h + 1)
                v.scalar_tensor_tensor(eb, zb, 0.0, eb, ALU.max, ALU.add).then_inc(s_sp, 1)

            def attend_back(h):
                zb = zs[:, h % 2, :]
                dve.wait_ge(s_cf, h + 1)
                v.tensor_tensor(zb, zb, cstick, ALU.subtract).then_inc(s_dd, 1)

            def attend_out(p):
                dve.wait_ge(s_pv, 2 * p + 2)
                v.tensor_copy(xnT[:, p, 0:TP], ps[:, 6 + p % 2, :]).then_inc(s_ot, 1)

            for h in range(SBH):
                attend_front(h)
                if h >= 2:
                    sum_keys(h - 2)
                if h >= 3 and h % 2:
                    attend_out((h - 3) // 2)
            attend_back(SBH - 1)
            sum_keys(SBH - 2)
            attend_out(3)
            sum_keys(SBH - 1)

            flat = lambda t: t.rearrange("p b f h -> p (b f h)")
            by_head = lambda t: t.rearrange("p b f h -> p (b f) h")
            dve.wait_ge(s_kused, TS)
            link(v.scalar_tensor_tensor(by_head(zz), by_head(zz), DH ** -0.5,
                                        sbb[:].unsqueeze(1).broadcast_to([P, TS * KEYS, SBH]), ALU.mult, ALU.add))
            v.scalar_tensor_tensor(flat(zl), flat(zz), -1.0, flat(zz), ALU.mult, ALU.min).then_inc(s_za, 1)
            dve.wait_ge(s_zw, 1)
            link(v.scalar_tensor_tensor(flat(zl), flat(zz), 0.0, flat(zl), ALU.max, ALU.add))
            link(v.tensor_copy(zr[:, :, KEYS - 1, :], zl[:, :, KEYS - 1, :]))
            for f in range(KEYS - 2, -1, -1):
                link(v.tensor_tensor(zr[:, :, f, :], zr[:, :, f + 1, :], zl[:, :, f, :], ALU.add))
            dve.sem_inc(s_zv, 1)
            link(v.tensor_tensor(flat(zz), flat(zz), flat(zr), ALU.subtract))
            s = drain_wait(dve, "cs", 0)
            later = s[:, 0, 0:TS * SBH].rearrange("p (b h) -> p b h", b=TS)
            v.tensor_tensor(zz, zz, later.unsqueeze(2).broadcast_to([P, TS, KEYS, SBH]), ALU.subtract
                            ).then_inc(s_drained["dve"], 1)
            dve.wait_ge(s_drained["dve"], JOBS[("cs", 0)][2])
            dve.sem_inc(s_za, 1)
            sums = slot(JOBS[("cs", 0)][0])
            for b in range(TS):
                dve.wait_ge(s_vused, b + 1)
                v.tensor_copy(vo[:, b, :], sums[0:SBH, b % 2, :]).then_inc(s_vo, 1)
            s = drain_wait(dve, "vs", 0)
            step = TS * SBH + 2
            own = [s[:, 0, c:c + 4 * step].rearrange("p (j x) -> p j x", j=4)[:, :, 0:TS * SBH:SBH] for c in range(2)]
            v.tensor_copy(xnT[0:64, 0:4, TP:T], own[0][0:64])
            v.tensor_copy(xnT[64:P, 0:4, TP:T], own[1][64:P]).then_inc(s_drained["dve"], 1)
            for m in range(4):
                s = drain_wait(dve, "poolproj", m)
                v.tensor_scalar(two(xnT[:, 4 + m, :]), halves(s), prm[:, P_SC + m:P_SC + m + 1], None, ALU.mult
                                ).then_inc(s_drained["dve"], 1)

            def add_to_h(name, i, m):
                s = drain_wait(dve, name, i)
                v.tensor_tensor(two(hT[:, m, :]), two(hT[:, m, :]), halves(s), ALU.add).then_inc(s_drained["dve"], 1)

            for m in range(KT):
                add_to_h("wout", m, m)
            norm(1, "wout", G_FFN)

            for layer in range(2):
                if layer:
                    norm(4, "woutc", G_FFN + 8)
                dve.wait_ge(s_rin, 64 * (layer + 1))
                dve.wait_ge(s_rc, layer + 1)
                b4 = lambda t: t.unsqueeze(2).broadcast_to([RT, NRT, 4])
                s = drain_wait(dve, "logits", layer)
                v.tensor_tensor(lg, s[0:RT, 0, 0:100].rearrange("p (i c) -> p i c", c=20),
                                br.unsqueeze(1).broadcast_to([RT, NRT, 20]), ALU.add).then_inc(s_drained["dve"], 1)
                dve.wait_ge(s_drained["dve"], JOBS[("logits", layer)][2])
                gl = lg[:, :, 0:NG]
                r5 = lambda n: rs[:, n, 0:NRT]
                r20 = lambda n: rs[:, n, :].rearrange("p (i c) -> p i c", c=4)
                pr = prio.unsqueeze(1).broadcast_to([RT, NRT, 4])

                def first_max(x, top, hot, t):
                    link(v.tensor_reduce(top, x, AX, ALU.max))
                    link(v.tensor_tensor(t, x, b4(top), ALU.is_equal))
                    link(v.tensor_tensor(t, t, pr, ALU.mult))
                    link(v.tensor_reduce(r5(9), t, AX, ALU.max))
                    link(v.tensor_tensor(hot, t, b4(r5(9)), ALU.is_equal))

                first_max(gl, r5(2), r20(3), r20(4))
                v.tensor_tensor(r20(0), gl, b4(r5(2)), ALU.subtract).then_inc(s_ri, 1)
                goh = r20(3).unsqueeze(3).broadcast_to([RT, NRT, NG, NPG])
                for g in range(NG):
                    link(v.tensor_tensor(mt[:, :, g, :], lg[:, :, NG + 4 * g:NG + 4 * g + 4],
                                         b4(r20(3)[:, :, g]), ALU.mult))
                link(v.tensor_reduce(r20(5), mt.rearrange("p i g e -> p i e g"), AX, ALU.add))
                first_max(r20(5), r5(6), r20(7), r20(4))
                link(v.scalar_tensor_tensor(r20(8), r20(7), -3e38, r20(5), ALU.mult, ALU.add))
                first_max(r20(8), r5(10), r20(11), r20(4))
                v.tensor_tensor(rs[:, 1, 0:NRT], r5(10), r5(6), ALU.subtract).then_inc(s_ri, 1)
                for mk, hot in ((m1, r20(7)), (m2, r20(11))):
                    for g in range(NG):
                        link(v.tensor_tensor(mk[:, :, g, :], hot, b4(r20(3)[:, :, g]), ALU.mult))
                f16 = lambda t: t.rearrange("p i g e -> p i (g e)")
                v.tensor_tensor(cnt, f16(m1), f16(m2), ALU.add).then_inc(s_cnt, 1)
                s = drain_wait(dve, "rank", layer)
                rank = s[0:RT, 0, 0:80].rearrange("p (i c) -> p i c", c=NE)
                rk = lambda n: rs[:, n, 0:10].rearrange("p (k i) -> p k i", k=2)
                ten = lambda n: rs[:, n, 0:10]
                for k, mk in enumerate((m1, m2)):
                    link(v.tensor_tensor(f16(mt), f16(mk), rank, ALU.mult))
                    link(v.tensor_reduce(rk(12)[:, k, :], f16(mt), AX, ALU.add))
                    link(v.tensor_tensor(f16(mt), f16(mk), io16.unsqueeze(1).broadcast_to([RT, NRT, NE]), ALU.mult))
                    link(v.tensor_reduce(rk(13)[:, k, :], f16(mt), AX, ALU.add))
                dve.sem_inc(s_drained["dve"], 1)
                link(v.tensor_scalar(ten(14), ten(12), float(CAP), None, ALU.is_ge))
                for n in range(2, BLK):
                    link(v.scalar_tensor_tensor(ten(14), ten(12), float(n * CAP), ten(14), ALU.is_ge, ALU.add))
                link(v.scalar_tensor_tensor(ten(15), ten(14), -float(CAP), ten(12), ALU.mult, ALU.add))
                link(v.scalar_tensor_tensor(ten(16), ten(13), float(BLK), ten(14), ALU.mult, ALU.add))
                link(v.tensor_reduce(rs[:, 17, 0:1], ten(14), AX, ALU.add))
                vl = vals.rearrange("p k i -> p (k i)")
                for n in range(10):
                    v.tensor_scalar(sel_c[:, n, :], iot, ten(15)[:, n:n + 1], None, ALU.is_equal)
                    ins = v.tensor_scalar(sel_b[:, n, :], iot[:, 0:NE * BLK], ten(16)[:, n:n + 1],
                                          vl[:, n:n + 1], ALU.is_equal, ALU.mult)
                ins.then_inc(s_sel, 1)
                dve.wait_ge(s_ro, 2 * layer + 2)
                link(v.tensor_reduce(r5(18), r20(0), AX, ALU.add))
                link(v.reciprocal(r5(18), r5(18)))
                link(v.tensor_scalar(r5(19), rs[:, 1, 0:NRT], 1.0, None, ALU.add))
                link(v.reciprocal(r5(19), r5(19)))
                link(v.tensor_tensor(wts[:, 0, :], r5(18), r5(19), ALU.mult))
                link(v.tensor_tensor(wts[:, 1, :], wts[:, 0, :], rs[:, 1, 0:NRT], ALU.mult))
                s = drain_wait(dve, "table", layer)
                link(v.tensor_scalar(tabf[:, 0, :], s[:, 0, 0:80], 0.0, UNUSED, ALU.is_equal, ALU.mult))
                link(v.scalar_tensor_tensor(tabf[:, 1, :], s[:, 0, 0:80], -1.0, tabf[:, 0, :], ALU.add, ALU.add))
                link(v.tensor_scalar(tabf[:, 2, :], tabf[:, 1, :], float(T), -float(T), ALU.is_ge, ALU.mult))
                link(v.tensor_tensor(tabf[:, 0, :], tabf[:, 1, :], tabf[:, 2, :], ALU.add))
                link(v.tensor_scalar(rs[0:1, 20, 0:1], s[0:1, 1, 0:1], 0.5, None, ALU.is_ge))
                link(v.tensor_copy(flag[:], rs[0:1, 20, 0:1]))
                link(v.tensor_copy(tab_i[:, 0, :], tabf[:, 0, :]))
                link(v.tensor_copy(tab_i[:, 1, :], tabf[:, 1, :]))
                dve.sem_inc(s_drained["dve"], 1)
                dve.sem_inc(s_tab, 1)
                by_pass = lambda t: t.rearrange("p (e r) -> p e r", e=NE)
                link(v.tensor_scalar(by_pass(taken[:, 0, :]), by_pass(tabf[0:1, 0, :])[:, :, 1:BLK], UNUSED / 2, None,
                                     ALU.is_lt))
                for k in range(2):
                    link(v.tensor_tensor(beyond[:, k, :, :], beyond[:, k, :, :], by_pass(taken[:, 0, :]), ALU.mult))
                far, n = 1, 0
                while far < NE * (BLK - 1):
                    link(v.tensor_copy(taken[:, 1 - n, 0:far], taken[:, n, 0:far]))
                    link(v.tensor_tensor(taken[:, 1 - n, far:], taken[:, n, far:], taken[:, n, 0:NE * (BLK - 1) - far],
                                         ALU.add))
                    far, n = 2 * far, 1 - n
                wide = [1, EXTRA, NE * (BLK - 1)]
                for k in range(2):
                    link(v.tensor_tensor(pick, taken[:, n, :].unsqueeze(1).broadcast_to(wide),
                                         iot[0:1, 1:EXTRA + 1].unsqueeze(2).broadcast_to(wide), ALU.is_equal))
                    link(v.tensor_tensor(pick, pick, beyond[:, k, :, :].rearrange("p e r -> p (e r)").unsqueeze(1)
                                         .broadcast_to(wide), ALU.mult))
                    link(v.tensor_reduce(picked, pick, AX, ALU.add))
                    link(v.tensor_copy(extra[:, k, :], picked))
                dve.sem_inc(s_tab, 1)

                u0 = FIRST_EXPERT[layer]

                def low_part(hu0, j):
                    dve.wait_ge(s_hi, NHU * layer + hu0 + 1 + 12 * j)
                    at = HU * (hu0 % 2)
                    w = unit(u0 + hu0 // 2)[:, at:at + HU]
                    w_lo = slots[(u0 + hu0 // 2) % RING][1][:, at:at + HU]
                    v.tensor_tensor(w_lo, w, high[hu0 % 4].bitcast(F32), ALU.subtract).then_inc(s_lo, 1)

                def turn_tokens(e, base=NE * layer):
                    dve.wait_ge(s_xt, base + e + 1)
                    v.tensor_tensor(xgT_lo, ps[:, 6:8, :].rearrange("p a (k c) -> p (a k) c", c=CAP),
                                    xgT_r.bitcast(F32), ALU.subtract).then_inc(s_xtl, 1)

                def hidden(e, base=NE * layer):
                    dve.wait_ge(s_hused, half_units("up", layer, e))
                    dve.wait_ge(s_sil, base + e + 1)
                    v.tensor_tensor(hid, sil, ps[:, 1, :], ALU.mult).then_inc(s_hid, 1)

                def expert_step(e0, j, last=False, base=NE * layer):
                    e, h = e0 + 2 * j, 6 * e0 + 2 if e0 else 4
                    low_part(h, j)
                    low_part(h + 1, j)
                    low_part(h + 2, j)
                    hidden(e)
                    low_part(h + 3, j)
                    if not last:
                        turn_tokens(e + 1)
                        if e0:
                            low_part(h + 4, j)
                            low_part(h + 5, j)
                    dve.wait_ge(s_ht, base + e + 1)
                    v.tensor_tensor(hidT_lo, ps[:, 4, :].rearrange("p (k c) -> p k c", c=CAP),
                                    hidT_r.bitcast(F32), ALU.subtract).then_inc(s_htl, 1)

                for hu in range(4):
                    low_part(hu, 0)
                turn_tokens(0)
                expert_step(0, 0)
                expert_step(1, 0)
                expert_step(2, 0)
                with dve.Fori(0, 6) as j:
                    expert_step(3, j)
                    expert_step(4, j)
                expert_step(15, 0, last=True)

                more = dve.value_load(flag[0:1, 0:1], min_val=0, max_val=1)
                o = ov[layer]
                with dve.If(more > 0):
                    with dve.Fori(0, EXTRA) as n:
                        column = dve.value_load(extra[0:1, 0, bass.ds(n, 1)], min_val=0, max_val=NE * BLK - 1)
                        with dve.If(column > 0):
                            dve.wait_ge(o["sil"], n + 1)
                            v.tensor_tensor(hid, sil, ps[:, 1, :], ALU.mult).then_inc(o["hid"], 1)
                            dve.wait_ge(o["df"], n + 1)
                            v.tensor_copy(yo[:, 0, :].rearrange("p (a b) -> p a b", a=2), ps[:, 2:4, :]
                                          ).then_inc(o["y"], 1)

                for i in range(NRT):
                    dve.wait_ge(s_yg[i], 16 * (layer + 1))
                    link(v.tensor_scalar(yg[:, i, 0:D], yg[:, i, 0:D], wts[:, 0, i:i + 1], None, ALU.mult))
                    v.scalar_tensor_tensor(yg[:, i, 0:D], yg[:, i, D:2 * D], wts[:, 1, i:i + 1], yg[:, i, 0:D],
                                           ALU.mult, ALU.add).then_inc(s_yc, 1)
                for d in range(KT):
                    s = drain_wait(dve, "combine", (layer, d))
                    v.tensor_tensor(hT[:, d, 0:416], hT[:, d, 0:416], s[:, 0, 0:416], ALU.add)
                    v.tensor_tensor(hT[:, d, 416:T], hT[:, d, 416:T], s[:, 1, 0:RT], ALU.add
                                    ).then_inc(s_drained["dve"], 1)

                norm(2 if layer == 0 else 5, f"moe{layer}", G_PG + 8 * layer)
                for m in range(KT):
                    s = drain_wait(dve, "pvalue", (layer, m))
                    dve.wait_ge(s_drained["act"], JOBS[("pgate", (layer, m))][2])
                    v.tensor_tensor(two(gv[:, m % 2, :]), two(sig[:, m % 2, :]), halves(s), ALU.mult
                                    ).then_inc(s_drained["dve"], 1)
                    dve.wait_ge(s_drained["dve"], JOBS[("pvalue", (layer, m))][2])
                    dve.sem_inc(s_sig, 1)
                    v.tensor_tensor(hT[:, m, :], hT[:, m, :], gv[:, m % 2, :], ALU.add).then_inc(s_h, 1)
                if layer:
                    break

                norm(3, "ple0", G_MIX + 8)
                for i in range(2):
                    s = drain_wait(dve, "chist", i)
                    for k in range(4):
                        c3 = chs[:, 4 * i + k, :].rearrange("p (b r) -> p b r", b=TS)
                        ins = v.tensor_copy(c3[:, :, 0:CHIST],
                                            s[:, k // 2, 240 * (k % 2):240 * (k % 2) + 240].rearrange(
                                                "p (b r) -> p b r", b=TS))
                    ins.then_inc(s_drained["dve"], 1)
                dve.wait_ge(s_cuz, 1)
                for m in range(KT):
                    s = drain_wait(dve, "ca", m)
                    dve.wait_ge(s_drained["act"], JOBS[("cg", m)][2])
                    link(v.tensor_tensor(cu[:, m, CPAD:CPAD + HALF], csig[:, m % 2, 0:HALF], s[:, 0, 0:HALF], ALU.mult))
                    link(v.tensor_tensor(cu[:, m, CPAD + HALF:CPAD + TP], csig[:, m % 2, HALF:TP],
                                         s[:, 1, 0:TP - HALF], ALU.mult))
                    c3 = chs[:, m, :].rearrange("p (b r) -> p b r", b=TS)
                    v.tensor_tensor(c3[:, :, CHIST], csig[:, m % 2, TP:T], s[:, 1, TP - HALF:HALF], ALU.mult
                                    ).then_inc(s_drained["dve"], 1)
                    dve.wait_ge(s_drained["dve"], JOBS[("ca", m)][2])
                    dve.sem_inc(s_cu, 1)
                for m in range(KT):
                    link(v.tensor_tensor(cprod.rearrange("p (b r) -> p b r", b=TS),
                                         chs[:, m, :].rearrange("p (b r) -> p b r", b=TS),
                                         wdw[:, m, :].unsqueeze(1).broadcast_to([P, TS, CW]), ALU.mult))
                    link(v.tensor_reduce(acc[:, m, TP:T], cprod.rearrange("p (b r) -> p b r", b=TS), AX, ALU.add))
                    link(v.tensor_scalar(acc[:, m, TP:T], acc[:, m, TP:T], prm[:, B_DW + m:B_DW + m + 1], None, ALU.add))
                for m in range(CONV_DVE):
                    link(v.tensor_scalar(acc[:, m, 0:TP], cu[:, m, 0:TP], wdw[:, m, 0:1],
                                         prm[:, B_DW + m:B_DW + m + 1], ALU.mult, ALU.add))
                    for c in range(1, CW):
                        link(v.scalar_tensor_tensor(acc[:, m, 0:TP], cu[:, m, c:c + TP], wdw[:, m, c:c + 1],
                                                    acc[:, m, 0:TP], ALU.mult, ALU.add))
                dve.sem_inc(s_acc, 1)
                dve.wait_ge(s_drained["act"], JOBS[("mean", 0)][2])
                for k in range(KT):
                    v.tensor_tensor(acc[:, k, :], acc[:, k, :], rms[:], ALU.subtract).then_inc(s_xc, 1)
                dve.wait_ge(s_drained["act"], JOBS[("var", 0)][2])
                link(v.reciprocal(rstd[:], rms[:]))
                for k in range(KT):
                    v.tensor_tensor(acc[:, k, :], acc[:, k, :], rstd[:], ALU.mult).then_inc(s_lnx, 1)
                for m in range(KT):
                    add_to_h("woutc", m, m)
            norm(6, "ple1", G_FIN)

        @block.tensor
        def _(pe):
            mm = nc.tensor.matmul

            def tr(dst, src, n):
                return nc.tensor.transpose(dst, src, ident[0:n, 0:n])

            def filled(ins):
                ins.then_inc(s_filled, 1)

            xn_seen = [0]

            def xn_wait(k):
                pe.wait_ge(s_xn, 8 * xn_seen[0] + k + 1)

            sq_seen = [0]

            def square_sums(name, i):
                s = fill_wait(pe, name, i)
                for k in range(KT):
                    pe.wait_ge(s_sq, 8 * sq_seen[0] + k + 1)
                    for half in range(2):
                        ins = mm(s[:, half, 0:HALF], ones[:], sq[:, k % 2, half * HALF:(half + 1) * HALF],
                                 start=(k == 0), stop=(k == KT - 1))
                    ins.then_inc(s_squsd if k < KT - 1 else s_filled, 1)
                sq_seen[0] += 1

            def channels(name, i, w, n, src=xnT, wait=None):
                s = fill_wait(pe, name, i)
                for k in range(n):
                    if wait:
                        wait(k)
                    for half in range(2):
                        ins = mm(s[:, half, 0:HALF], w[:, k, :], src[:, k, half * HALF:(half + 1) * HALF],
                                 start=(k == 0), stop=(k == n - 1))
                filled(ins)

            pe.wait_ge(s_const, 1)
            pe.wait_ge(s_in, 32)
            for i in range(4):
                s = fill_wait(pe, "x", i)
                for k in range(2):
                    for t in range(4):
                        ins = tr(s[:, k, t * P:(t + 1) * P], x_tok[:, t, (2 * i + k) * P:(2 * i + k + 1) * P], P)
                filled(ins)
            s = fill_wait(pe, "x", 4)
            pe.wait_ge(s_in2, 16 * 12)
            for k in range(KT):
                tr(s[:, 0, k * TS:(k + 1) * TS], x_smp[:, k * P:(k + 1) * P], TS)
            tr(s[:, 1, 0:N_PRM], prm_rows, N_PRM)
            for k in range(KT):
                ins = tr(s[:, 1, 128 + k * CW:128 + (k + 1) * CW], dw_rows[:, k * P:(k + 1) * P], CW)
            filled(ins)

            square_sums("norm", 0)
            for name, c in (("q", 0), ("k", 1)):
                unit_wait(pe, c)
                for m in range(4):
                    channels(name, m, w_view(c)[:, :, m * P:(m + 1) * P], KT, wait=xn_wait)
            unit_wait(pe, 2)
            for i in range(3):
                s = fill_wait(pe, "v", i)
                for b in range(2 if i < 2 else 1):
                    t = 2 * i + b
                    rows = P if t < 4 else TS
                    for k in range(KT):
                        ins = mm(s[0:rows, b, :], xnT[:, k, t * P:t * P + rows], w_view(2)[:, k, :],
                                 start=(k == 0), stop=(k == KT - 1))
                filled(ins)
            unit_wait(pe, 3)
            for m in range(4):
                channels("u", m, w_view(3)[:, :, m * P:(m + 1) * P], KT)
            xn_seen[0] += 1

            s = fill_wait(pe, "qrow", 0)
            pe.wait_ge(s_drained["act"], JOBS[("q", 3)][2])
            pe.wait_ge(s_drained["dve"], JOBS[("u", 3)][2])
            for m in range(4):
                tr(s[0:TS, 0, m * P:(m + 1) * P], qT[:, m, TP:T], P)
                ins = tr(s[0:TS, 1, m * P:(m + 1) * P], up[:, m, PAD + TP:PAD + T], P)
            filled(ins)
            for i in range(3):
                s = fill_wait(pe, "krow", i)
                for b in range(2 if i < 2 else 1):
                    t = 2 * i + b
                    rows = P if t < 4 else TS
                    for m in range(4):
                        ins = tr(s[0:rows, b, m * P:(m + 1) * P], kT[:, m, t * P:t * P + rows], P)
                filled(ins)
            s = fill_wait(pe, "urow", 0)
            pe.wait_ge(s_hist, 16)
            for m in range(4):
                tr(s[0:HIST, 0, m * P:(m + 1) * P], up[:, m, PAD + TP - HIST:PAD + TP], P)
                ins = tr(s[:, 1, m * 120:(m + 1) * 120], hist_rows[:, m * P:(m + 1) * P], 120)
            filled(ins)

            all_drained(pe, "urow", 0)
            at = {0: 0, 1: 512, 3: 896, 2: 1024}
            z0, c0 = 0, 1536

            def scores(h):
                rows = slice(64 * (h % 2), 64 * (h % 2) + 64)
                if h:
                    pe.wait_ge(s_zs, h)
                for kb in range(4):
                    ins = mm(ps_flat[:, z0 + at[kb]:z0 + at[kb] + TP - kb * P],
                             kT[rows, h // 2, kb * P:(kb + 1) * P], qT[rows, h // 2, kb * P:TP],
                             start=True, stop=True)
                ins.then_inc(s_zf, 1)

            def sticks(h):
                pe.wait_ge(s_spm, h + 1)
                if h:
                    pe.wait_ge(s_dd, h)
                sp = ex[:, h % 2, :]
                for kb in range(4):
                    for src in range(kb, 4):
                        off = (src - kb) * P
                        width = TP - src * P
                        ins = mm(ps_flat[:, c0 + at[kb] + off:c0 + at[kb] + off + width],
                                 tri[:] if src == kb else ones[:], sp[:, at[src]:at[src] + width],
                                 start=(src == kb), stop=(src == 3), skip_group_check=True)
                ins.then_inc(s_cf, 1)

            def values(h):
                pe.wait_ge(s_wm, h + 1)
                if h >= 4 and h % 2 == 0:
                    pe.wait_ge(s_ot, h // 2 - 1)
                rows = slice(64 * (h % 2), 64 * (h % 2) + 64)
                for kb in range(4):
                    ins = mm(ps[rows, 6 + (h // 2) % 2, kb * P:TP], v_tok[:, kb, h * DH:(h + 1) * DH],
                             zs[:, h % 2, at[kb]:at[kb] + TP - kb * P], start=(kb == 0), stop=(kb == 3),
                             skip_group_check=True)
                ins.then_inc(s_pv, 1)

            scores(0)
            for h in range(SBH):
                if h + 1 < SBH:
                    scores(h + 1)
                if h:
                    values(h - 1)
                sticks(h)
            values(SBH - 1)

            pe.wait_ge(s_dd, SBH)
            pe.wait_ge(s_ot, 4)
            pe.wait_ge(s_zs, SBH)
            s = slot(JOBS[("cs", 0)][0])
            pe.wait_ge(s_zv, 1)
            filled(mm(s[:, 0, 0:TS * SBH], after[:], zr[:, :, 0, :], start=True, stop=True))
            out_s, s = s, slot(JOBS[("vs", 0)][0])
            pe.wait_ge(s_zw, 2)

            def turn_sample(b):
                pe.wait_ge(s_vo, b + 1)
                for j in range(4):
                    at = (j * TS + b) * SBH
                    ins = tr(s[:, 0, at:at + SBH], vo[:, b, j * P:(j + 1) * P], SBH)
                return ins

            for b in range(TS):
                n = UNIT[("v", b)]
                unit_wait(pe, n)
                rows = unit(n).rearrange("p (f c) -> p f c", f=KEYS)
                for f in range(KEYS):
                    ins = mm(out_s[0:SBH, b % 2, :], zz[:, b, f, :], rows[:, f, :], start=(f == 0), stop=(f == KEYS - 1))
                ins.then_inc(s_vused, 1)
                if b:
                    turn_sample(b - 1)
            filled(turn_sample(TS - 1))

            pe.wait_ge(s_pooled, 1)
            for m in range(4):
                channels("poolproj", m, wpool[:, m:m + 1, :], 1, src=up[:, m:m + 1, PAD:PAD + T])
            for c in range(2):
                n = UNIT[("w_out_ab", c)]
                unit_wait(pe, n)
                for m in range(4):
                    channels("wout", 4 * c + m, w_view(n)[:, :, m * P:(m + 1) * P], KT,
                             wait=(lambda k: pe.wait_ge(s_drained["dve"], JOBS[("poolproj", 3)][2]) if k == 4 else
                                   pe.wait_ge(s_drained["dve"], JOBS[("vs", 0)][2])) if not c and not m else None)

            square_sums("norm", 1)
            for layer in range(2):
                if layer:
                    square_sums("norm", 4)
                s = fill_wait(pe, "logits", layer)
                pe.wait_ge(s_rin, 64 * (layer + 1))
                for i in range(NRT):
                    for k in range(KT):
                        xn_wait(k)
                        ins = mm(s[0:RT, 0, i * 20:(i + 1) * 20], xnT[:, k, i * RT:(i + 1) * RT], wr[:, k, :],
                                 start=(k == 0), stop=(k == KT - 1))
                filled(ins)
                xn_seen[0] += 1
                for i in range(NRT):
                    s = fill_wait(pe, "rows", (layer, i))
                    for k in range(KT):
                        ins = tr(s[0:RT, k // 4, (k % 4) * P:(k % 4 + 1) * P], xnT[:, k, i * RT:(i + 1) * RT], P)
                    filled(ins)
                s = fill_wait(pe, "rank", layer)
                pe.wait_ge(s_cnt, layer + 1)
                for i in range(NRT):
                    for src in range(i + 1):
                        ins = mm(s[0:RT, 0, i * NE:(i + 1) * NE],
                                 before[0:RT, 0:RT] if src == i else ones[0:RT, 0:RT], cnt[:, src, :],
                                 start=(src == 0), stop=(src == i))
                filled(ins)
                s = fill_wait(pe, "table", layer)
                pe.wait_ge(s_sel, layer + 1)
                for n in range(10):
                    mm(s[:, 0, 0:NE * BLK], sel_c[:, n, :], sel_b[:, n, :], start=(n == 0), stop=(n == 9))
                filled(mm(s[0:1, 1, 0:1], ones[0:RT, 0:1], rs[:, 17, 0:1], start=True, stop=True))

                all_drained(pe, "table", layer)
                u0 = FIRST_EXPERT[layer]

                def turn_tokens(e, par, j, base=NE * layer):
                    pe.wait_ge(s_xg[par], 16 * ((NE // 2) * layer + j + 1))
                    if not isinstance(e, int) or base + e:
                        pe.wait_ge(s_xtl, base + e)
                    for k in range(KT):
                        ins = tr(ps[:, 6 + k // 4, (k % 4) * P:(k % 4 + 1) * P], xg[:, par, k * P:(k + 1) * P], P)
                    ins.then_inc(s_xtf, 1)

                def parts_product(bank, x, x_lo, w, w_lo, start, stop):
                    mm(ps[:, bank, :], x, w, start=start, stop=False)
                    mm(ps[:, bank, :], x, w_lo, start=False, stop=False)
                    return mm(ps[:, bank, :], x_lo, w, start=False, stop=stop)

                def gate_up(e, hu0, j, base=NE * layer):
                    pe.wait_ge(s_xtl, base + e + 1)
                    if not isinstance(e, int) or base + e:
                        pe.wait_ge(s_hid, base + e)
                    for hu in range(hu0, hu0 + 4):
                        pe.wait_ge(s_lo, NHU * layer + hu + 1 + 12 * j)
                        hi = high[hu % 4].rearrange("p (k c) -> p k c", c=F)
                        lo = slots[(u0 + hu // 2) % RING][1][:].rearrange("p (k c) -> p k c", k=KT)
                        for k in range(4):
                            kk = 4 * (hu % 2) + k
                            ins = parts_product((hu - hu0) // 2, xgT_r[:, kk, :], xgT_lo[:, kk, :], hi[:, k, :],
                                                lo[:, kk, :], kk == 0, kk == KT - 1)
                        ins.then_inc(s_hused, 1)

                def turn_hidden(e, base=NE * layer):
                    pe.wait_ge(s_hid, base + e + 1)
                    if not isinstance(e, int) or base + e:
                        pe.wait_ge(s_htl, base + e)
                    for k in range(FT):
                        ins = tr(ps[:, 4, k * P:(k + 1) * P], hid[:, k * P:(k + 1) * P], P)
                    ins.then_inc(s_htf, 1)

                def down(e, hu0, j, base=NE * layer):
                    pe.wait_ge(s_htl, base + e + 1)
                    if not isinstance(e, int) or base + e:
                        pe.wait_ge(s_y, base + e)
                    for hu in range(hu0, hu0 + 2):
                        pe.wait_ge(s_lo, NHU * layer + hu + 1 + 12 * j)
                        hi = high[hu % 4].rearrange("p (k c) -> p k c", c=D)
                        lo = slots[(u0 + hu // 2) % RING][1][:].rearrange("p (k c) -> p k c", k=FT)
                        for k in range(2):
                            kk = 2 * (hu % 2) + k
                            for b in range(2):
                                cols = slice(b * 512, b * 512 + 512)
                                ins = parts_product(2 + b, hidT_r[:, kk, :], hidT_lo[:, kk, :], hi[:, k, cols],
                                                    lo[:, kk, cols], kk == 0, kk == FT - 1)
                        ins.then_inc(s_hused, 1)

                def expert_step(e0, j, last=False):
                    e = e0 + 2 * j
                    gate_up(e, 6 * e0 - 2, j)
                    if not last:
                        turn_tokens(e + 1, (e0 + 1) % 2, (e0 + 1) // 2 + j)
                    down(e - 1, 6 * e0 + 2, j)
                    turn_hidden(e)

                turn_tokens(0, 0, 0)
                gate_up(0, 0, 0)
                turn_tokens(1, 1, 0)
                turn_hidden(0)
                expert_step(1, 0)
                expert_step(2, 0)
                with pe.Fori(0, 6) as j:
                    expert_step(3, j)
                    expert_step(4, j)
                expert_step(15, 0, last=True)
                down(15, NHU - 2, 0)

                pe.wait_ge(s_tab, 2 * layer + 2)
                more = pe.value_load(flag[0:1, 0:1], min_val=0, max_val=1)
                o = ov[layer]
                with pe.If(more > 0):
                    pe.wait_ge(s_y, NE * (layer + 1))
                    pe.wait_ge(s_hused, NHU * (layer + 1))
                    pe.sem_inc(o["eused"], 1)
                    with pe.Fori(0, EXTRA) as n:
                        column = pe.value_load(extra[0:1, 0, bass.ds(n, 1)], min_val=0, max_val=NE * BLK - 1)
                        with pe.If(column > 0):
                            pe.wait_ge(o["xg"], 16 * n + 16)
                            for k in range(KT):
                                ins = tr(ps[:, 6 + k // 4, (k % 4) * P:(k % 4 + 1) * P], xg[:, 0, k * P:(k + 1) * P], P)
                            ins.then_inc(o["xtf"], 1)
                            pe.wait_ge(o["land"], 48 * n + 48)
                            pe.wait_ge(o["xt"], n + 1)
                            for b in range(2):
                                for k in range(KT):
                                    ins = mm(ps[:, b, :], xgT[:, k, :], w_view(b)[:, k, :],
                                             start=(k == 0), stop=(k == KT - 1))
                            ins.then_inc(o["guf"], 1)
                            pe.wait_ge(o["hid"], n + 1)
                            for k in range(FT):
                                ins = tr(ps[:, 4, k * P:(k + 1) * P], hid[:, k * P:(k + 1) * P], P)
                            ins.then_inc(o["htf"], 1)
                            pe.wait_ge(o["ht"], n + 1)
                            w = unit(2).rearrange("p (k c) -> p k c", k=FT)
                            for b in range(2):
                                for k in range(FT):
                                    ins = mm(ps[:, 2 + b, :], hidT[:, k, :], w[:, k, b * 512:(b + 1) * 512],
                                             start=(k == 0), stop=(k == FT - 1))
                            ins.then_inc(o["df"], 1)
                            pe.wait_ge(o["y"], n + 1)
                            pe.sem_inc(o["eused"], 1)

                for d in range(KT):
                    s = slot(JOBS[("combine", (layer, d))][0])
                    if d >= 4:
                        fill_wait(pe, "combine", (layer, d))
                    else:
                        pe.wait_ge(s_y, NE * (layer + 1))
                    for i in range(NRT):
                        if not d:
                            pe.wait_ge(s_yc, NRT * layer + i + 1)
                        ins = tr(s[:, i // 4, (i % 4) * RT:(i % 4 + 1) * RT], yg[:, i, d * P:(d + 1) * P], RT)
                    filled(ins)

                square_sums("norm", 2 if layer == 0 else 5)
                s = fill_wait(pe, "pT", (layer, 0))
                pe.wait_ge(s_pin[0], 16 * (layer + 1))
                for k in range(2):
                    for t in range(4):
                        ins = tr(s[:, k, t * P:(t + 1) * P], p_tok[:, t, k * P:(k + 1) * P], P)
                filled(ins)
                s = fill_wait(pe, "pT", (layer, 1))
                pe.wait_ge(s_pin[1], 16 * (layer + 1))
                for k in range(2):
                    ins = tr(s[:, 0, k * TS:(k + 1) * TS], p_smp[:, k * P:(k + 1) * P], TS)
                filled(ins)
                nv = UNIT[("w_ple", layer)]
                for m in range(KT):
                    n = UNIT[("w_pg", layer, m // 4)]
                    unit_wait(pe, n)
                    channels("pgate", (layer, m), w_view(n)[:, :, (m % 4) * P:(m % 4 + 1) * P], KT, wait=xn_wait)
                    unit_wait(pe, nv)
                    pe.wait_ge(s_drained["act"], JOBS[("pT", (layer, 1))][2])
                    channels("pvalue", (layer, m), ple_view(nv)[:, :, m * P:(m + 1) * P], 2, src=pT)
                xn_seen[0] += 1
                if layer:
                    break

                square_sums("norm", 3)
                pe.wait_ge(s_cin, 32)
                for i in range(2):
                    s = fill_wait(pe, "chist", i)
                    for k in range(4):
                        for g in range(2):
                            off = 240 * (k % 2) + 120 * g
                            ins = tr(s[:, k // 2, off:off + 120], ch_rows[:, g, (4 * i + k) * P:(4 * i + k + 1) * P], 120)
                    filled(ins)
                for m in range(KT):
                    na, ng = UNIT[("w_in_c", m // 4)], UNIT[("w_in_c", 2 + m // 4)]
                    unit_wait(pe, ng)
                    cols = slice((m % 4) * P, (m % 4 + 1) * P)
                    channels("cg", m, w_view(ng)[:, :, cols], KT, wait=xn_wait)
                    unit_wait(pe, na)
                    channels("ca", m, w_view(na)[:, :, cols], KT)
                xn_seen[0] += 1
                pe.wait_ge(s_cu, KT)
                s = fill_wait(pe, "crow", 0)
                for k in range(KT):
                    ins = tr(s[0:CHIST, k // 4, (k % 4) * P:(k % 4 + 1) * P], cu[:, k, TP:TP + CPAD], P)
                filled(ins)
                s = fill_wait(pe, "csrow", 0)
                for k in range(KT):
                    c3 = chs[:, k, :].rearrange("p (b r) -> p b r", b=TS)
                    ins = tr(s[0:TS, k // 4, (k % 4) * P:(k % 4 + 1) * P], c3[:, :, CHIST], P)
                filled(ins)
                n = 0
                for m in range(CONV_DVE, KT):
                    s = fill_wait(pe, "conv", m)
                    for c in range(CW):
                        pe.wait_ge(s_diag, n + 1)
                        mm(s[:, 0, :], diag[:, n % 4, :], cu[:, m, c:c + TP], start=(c == 0), stop=(c == CW - 1)
                           ).then_inc(s_dused, 1)
                        n += 1
                    pe.wait_ge(s_dused, n)
                    pe.sem_inc(s_filled, 1)
                s = fill_wait(pe, "mean", 0)
                pe.wait_ge(s_acc, 1)
                pe.wait_ge(s_drained["act"], JOBS[("conv", KT - 1)][2])
                for k in range(KT):
                    for half in range(2):
                        ins = mm(s[:, half, 0:HALF], ones[:], acc[:, k, half * HALF:(half + 1) * HALF],
                                 start=(k == 0), stop=(k == KT - 1))
                filled(ins)
                square_sums("var", 0)
                for c in range(2):
                    n = UNIT[("w_out_c", c)]
                    unit_wait(pe, n)
                    for m in range(4):
                        channels("woutc", 4 * c + m, w_view(n)[:, :, m * P:(m + 1) * P], KT,
                                 wait=lambda k: pe.wait_ge(s_silu, k + 1))

            square_sums("norm", 6)
            for i in range(5):
                s = fill_wait(pe, "y", i)
                rows = P if i < 4 else TS
                for k in range(KT):
                    xn_wait(k)
                    ins = tr(s[0:rows, k // 4, (k % 4) * P:(k % 4 + 1) * P], xnT[:, k, i * P:i * P + rows], P)
                filled(ins)


_INS = ['x_prompt', 'x_sample', 'p_prompt', 'p_sample', 'cache_k', 'cache_v', 'state_pool', 'state_conv', 'page_table',
        'norm_mix', 'norm_ffn', 'norm_final', 'w_in_ab', 'sb_bias', 'w_pool', 'pool_scale', 'w_out_ab', 'w_in_c',
        'w_dw', 'b_dw', 'ln_g_c', 'ln_b_c', 'w_out_c', 'w_rg', 'b_rg', 'w_re', 'b_re', 'w_gate_e', 'w_up_e',
        'w_down_e', 'w_ple', 'w_ple_gate', 'b_ple_gate', 'g_ple_gate']
_OUTS = [('y_prompt', (1, 512, 1024)), ('y_sample', (8, 1, 1024)), ('k_prompt', (1, 1, 512, 8, 64)),
         ('v_prompt', (1, 1, 512, 8, 64)), ('pool_prompt', (1, 1, 15, 512)), ('conv_prompt', (1, 1, 30, 1024)),
         ('k_sample', (1, 8, 1, 8, 64)), ('v_sample', (1, 8, 1, 8, 64)), ('pool_sample', (1, 8, 15, 512)),
         ('conv_sample', (1, 8, 30, 1024))]


def kernel(**inputs):
    import numpy as _np
    import concourse.bacc as _bacc
    from concourse import mybir as _mybir
    from concourse.bass_utils import run_bass_kernel_spmd as _run

    nc = _bacc.Bacc("TRN2", target_bir_lowering=False, num_devices=1)
    arrays, a, out = {}, {}, {}
    for name in _INS:
        x = _np.ascontiguousarray(inputs[name])
        arrays[f"in_{name}"] = x
        a[name] = nc.dram_tensor(f"in_{name}", x.shape, _mybir.dt.from_np(x.dtype), kind="ExternalInput").ap()
    for name, shape in _OUTS:
        out[name] = nc.dram_tensor(f"out_{name}", shape, _mybir.dt.float32, kind="ExternalOutput").ap()
    decoder_step(nc, a, out)
    r = _run(nc, [arrays], core_ids=[0])
    return tuple(r.results[0][f"out_{name}"] for name, _ in _OUTS)
```
